# Optimizing a Trainium2 kernel written in Bass

```python
import math
import jax, jax.numpy as jnp
from jax import lax
import numpy as np

D_MODEL = 1024
BATCH = 1
SEQ = 256
DEPTH = 1
DEC_BATCH = 8
DEC_SEQ = 1
PAST_LEN = 1024
PAGE_SIZE = 128

HEAD_DIM = 64
A_HEADS = 8
A_WIDTH = A_HEADS * HEAD_DIM
A_DECAY_RANK = 64
A_ICLR_RANK = 64
A_GATE_RANK = 128
A_GN_EPS = 64e-5
B_HEADS = 8
B_KV_HEADS = 2
B_GROUP = B_HEADS // B_KV_HEADS
B_WIDTH = B_HEADS * HEAD_DIM
KV_WIDTH = B_KV_HEADS * HEAD_DIM
CMP_BLOCK = 32
CMP_HIDDEN = 128
SEL_BLOCK = 64
SEL_RATIO = SEL_BLOCK // CMP_BLOCK
TOP_N = 16
WINDOW = 512
Q_BLOCK = 128
FORCE_SCORE = 1e4
N_BUCKETS = 32
MAX_EXACT = N_BUCKETS // 2
MAX_DISTANCE = 1024
N_EXPERTS = 32
TOP_K = 4
D_FF = 1024
SWIGLU_ALPHA = 1.702
SWIGLU_LIMIT = 7.0
MOE_CHUNK = 128
NORM_EPS = 1e-6
NEG_INF = -1e30
A_COLS = (A_WIDTH, A_WIDTH, A_WIDTH, A_DECAY_RANK, A_ICLR_RANK, A_GATE_RANK)
A_PROJ = 3 * A_WIDTH + A_DECAY_RANK + A_ICLR_RANK + A_GATE_RANK
B_PROJ = B_WIDTH + 6 * KV_WIDTH + 3 * B_HEADS
GATE_PROJ = 2 * D_MODEL
MIX_COLS = (A_PROJ, B_PROJ, GATE_PROJ)
P_TOTAL = A_PROJ + B_PROJ + GATE_PROJ

kernel_name = 'hybrid_rwkv7_nsa_moe_step'

def split_cols(p, sizes):
    return jnp.split(p, [int(i) for i in np.cumsum(sizes)[:-1]], axis=-1)

def rms_norm(x, g):
    xf = x.astype(jnp.float32)
    y = xf * lax.rsqrt(jnp.mean(xf * xf, axis=-1, keepdims=True) + NORM_EPS)
    return (y * g.astype(jnp.float32)).astype(x.dtype)

def rel_bucket(dist):
    n = jnp.maximum(dist, 0)
    log_ratio = jnp.log(jnp.maximum(n, 1).astype(jnp.float32) / MAX_EXACT) / math.log(MAX_DISTANCE / MAX_EXACT)
    large = jnp.minimum(MAX_EXACT + (log_ratio * (N_BUCKETS - MAX_EXACT)).astype(jnp.int32), N_BUCKETS - 1)
    return jnp.where(n < MAX_EXACT, n, large)

def rel_bias_heads(rel_bias, dist):
    b = rel_bias.astype(jnp.float32)[rel_bucket(dist)]
    return jnp.moveaxis(b, -1, 0).reshape(B_KV_HEADS, B_GROUP, *dist.shape)

def wkv7_scan(s0, r, w, k, v, a, b):
    def step(s, z):
        r_t, w_t, k_t, v_t, a_t, b_t = z
        sa = jnp.einsum('bhij,bhj->bhi', s, a_t)
        s = s * w_t[:, :, None, :] + sa[..., None] * b_t[:, :, None, :] + v_t[..., None] * k_t[:, :, None, :]
        return s, jnp.einsum('bhij,bhj->bhi', s, r_t)
    xs = tuple(jnp.moveaxis(z, 1, 0) for z in (r, w, k, v, a, b))
    s_fin, ys = lax.scan(step, s0, xs)
    return s_fin, jnp.moveaxis(ys, 0, 1)

def rwkv_branch(p_a, prev_row, s0, mu_shift, w0, w_decay_up, a0, w_iclr_up, w_gate_up, k_k, k_a, r_k, ln_x_w, ln_x_b):
    b, t, _ = p_a.shape
    f32 = jnp.float32
    prev = jnp.concatenate([prev_row[:, None].astype(p_a.dtype), p_a[:, :-1]], axis=1)
    ps = p_a + mu_shift * (prev - p_a)
    r, k, v, xw, xa, xg = split_cols(ps, A_COLS)
    heads = lambda z: z.reshape(b, t, A_HEADS, HEAD_DIM)
    w_log = -jax.nn.softplus(-(w0.astype(f32) + jnp.tanh(xw.astype(f32)) @ w_decay_up.astype(f32))) - 0.5
    decay = jnp.exp(-jnp.exp(w_log))
    a = jax.nn.sigmoid(a0.astype(f32) + xa.astype(f32) @ w_iclr_up.astype(f32))
    gate = jax.nn.sigmoid(xg) @ w_gate_up
    k = k.astype(f32)
    kk = heads(k * k_k.astype(f32))
    kk = kk / jnp.maximum(jnp.sqrt(jnp.sum(kk * kk, axis=-1, keepdims=True)), 1e-12)
    k = heads(k * (1.0 + (a - 1.0) * k_a.astype(f32)))
    r, v, a = heads(r.astype(f32)), heads(v.astype(f32)), heads(a)
    s_fin, y = wkv7_scan(s0.astype(f32), r, heads(decay), k, v, -kk, kk * a)
    mu = jnp.mean(y, axis=-1, keepdims=True)
    var = jnp.mean(jnp.square(y - mu), axis=-1, keepdims=True)
    y = ((y - mu) * lax.rsqrt(var + A_GN_EPS)).reshape(b, t, A_WIDTH) * ln_x_w.astype(f32) + ln_x_b.astype(f32)
    y = y + (jnp.sum(r * k * r_k.astype(f32), axis=-1, keepdims=True) * v).reshape(b, t, A_WIDTH)
    return y.astype(p_a.dtype) * gate, s_fin.astype(s0.dtype), p_a[:, -1]

def nsa_split(p_b):
    b, t = p_b.shape[:2]
    q, kv, gate = split_cols(p_b, (B_WIDTH, 6 * KV_WIDTH, 3 * B_HEADS))
    return (q.reshape(b, t, B_HEADS, HEAD_DIM),
            kv.reshape(b, t, 3, 2, B_KV_HEADS, HEAD_DIM),
            jax.nn.sigmoid(gate).reshape(b, t, B_HEADS, 3))

def compress_branch(cmp_kv, pe_k, pe_v, w_k1, w_k2, w_v1, w_v2):
    b, L = cmp_kv.shape[:2]
    nc = L // CMP_BLOCK
    blk = cmp_kv[:, :nc * CMP_BLOCK].reshape(b, nc, CMP_BLOCK, 2, B_KV_HEADS, HEAD_DIM)
    def phi(x, pe, w1, w2):
        flat = (x + pe[:, None, :]).transpose(0, 1, 3, 2, 4).reshape(b, nc, B_KV_HEADS, CMP_BLOCK * HEAD_DIM)
        return jax.nn.gelu(flat @ w1) @ w2
    cmp_end = jnp.arange(nc) * CMP_BLOCK + (CMP_BLOCK - 1)
    return phi(blk[:, :, :, 0], pe_k, w_k1, w_k2), phi(blk[:, :, :, 1], pe_v, w_v1, w_v2), cmp_end

def sel_blocks(sel_kv):
    b, L = sel_kv.shape[:2]
    ns = -(-L // SEL_BLOCK)
    x = jnp.pad(sel_kv, ((0, 0), (0, ns * SEL_BLOCK - L), (0, 0), (0, 0), (0, 0)))
    x = x.reshape(b, ns, SEL_BLOCK, 2, B_KV_HEADS, HEAD_DIM).transpose(3, 0, 4, 1, 2, 5)
    return x[0], x[1]

def nsa_attend(q, pos, gates, cmp_k, cmp_v, cmp_end, sel_k, sel_v, win_k, win_v, win_pos, rel_bias):
    b, qb = q.shape[:2]
    ns = sel_k.shape[2]
    scale = HEAD_DIM ** -0.5
    qg = q.reshape(b, qb, B_KV_HEADS, B_GROUP, HEAD_DIM)
    d_c = pos[:, None] - cmp_end[None, :]
    ok_c = d_c >= 0
    s_c = jnp.einsum('bqgrd,bngd->bgrqn', qg, cmp_k).astype(jnp.float32) * scale + rel_bias_heads(rel_bias, d_c)
    p_c = jax.nn.softmax(jnp.where(ok_c, s_c, NEG_INF), axis=-1) * ok_c
    o_c = jnp.einsum('bgrqn,bngd->bqgrd', p_c.astype(q.dtype), cmp_v)
    imp = jnp.sum(p_c, axis=2)
    imp = jnp.pad(imp, ((0, 0), (0, 0), (0, 0), (0, SEL_RATIO * ns - imp.shape[-1])))
    imp = imp.reshape(b, B_KV_HEADS, qb, ns, SEL_RATIO).sum(axis=-1)
    blk = jnp.arange(ns)[None, :]
    cur = (pos // SEL_BLOCK)[:, None]
    forced = (blk == 0) | (blk == cur) | (blk == cur - 1)
    score = jnp.where(blk <= cur, imp + FORCE_SCORE * forced, NEG_INF)
    top_val, top_idx = lax.top_k(score, min(TOP_N, ns))
    top_ok = top_val > NEG_INF / 2
    bi = jnp.arange(b)[:, None, None, None]
    gi = jnp.arange(B_KV_HEADS)[None, :, None, None]
    k_sel = sel_k[bi, gi, top_idx]
    v_sel = sel_v[bi, gi, top_idx]
    d_s = pos[:, None, None] - (top_idx[..., None] * SEL_BLOCK + jnp.arange(SEL_BLOCK))
    ok_s = (top_ok[..., None] & (d_s >= 0))[:, :, None]
    tbl = rel_bias.astype(jnp.float32).reshape(N_BUCKETS, B_KV_HEADS, B_GROUP)
    b_s = jnp.moveaxis(tbl[rel_bucket(d_s), gi[..., None]], -1, 2)
    s_s = jnp.einsum('bqgrd,bgqksd->bgrqks', qg, k_sel).astype(jnp.float32) * scale + b_s
    shp = s_s.shape
    p_s = jax.nn.softmax(jnp.where(ok_s, s_s, NEG_INF).reshape(*shp[:4], -1), axis=-1).reshape(shp)
    o_s = jnp.einsum('bgrqks,bgqksd->bqgrd', p_s.astype(q.dtype), v_sel)
    d_w = pos[:, None] - win_pos[None, :]
    ok_w = (d_w >= 0) & (d_w < WINDOW) & (win_pos[None, :] >= 0)
    s_w = jnp.einsum('bqgrd,bwgd->bgrqw', qg, win_k).astype(jnp.float32) * scale + rel_bias_heads(rel_bias, d_w)
    p_w = jax.nn.softmax(jnp.where(ok_w, s_w, NEG_INF), axis=-1)
    o_w = jnp.einsum('bgrqw,bwgd->bqgrd', p_w.astype(q.dtype), win_v)
    g = gates.reshape(b, qb, B_KV_HEADS, B_GROUP, 3)
    o = g[..., 0:1] * o_c + g[..., 1:2] * o_s + g[..., 2:3] * o_w
    return o.reshape(b, qb, B_WIDTH)

def nsa_prompt(p_b, cmp_w, rel_bias):
    q, kv, gates = nsa_split(p_b)
    b, t = q.shape[:2]
    cmp_k, cmp_v, cmp_end = compress_branch(kv[:, :, 0], *cmp_w)
    sel_k, sel_v = sel_blocks(kv[:, :, 1])
    win_pad = jnp.pad(kv[:, :, 2], ((0, 0), (WINDOW, 0), (0, 0), (0, 0), (0, 0)))
    def one_block(start):
        take = lambda z, n: lax.dynamic_slice_in_dim(z, start, n, axis=1)
        w_kv = take(win_pad, Q_BLOCK + WINDOW)
        return nsa_attend(take(q, Q_BLOCK), start + jnp.arange(Q_BLOCK), take(gates, Q_BLOCK),
                          cmp_k, cmp_v, cmp_end, sel_k, sel_v, w_kv[:, :, 0], w_kv[:, :, 1],
                          start - WINDOW + jnp.arange(Q_BLOCK + WINDOW), rel_bias)
    y = lax.map(one_block, jnp.arange(0, t, Q_BLOCK))
    y = jnp.moveaxis(y, 0, 1).reshape(b, t, B_WIDTH)
    n_win = min(WINDOW, t)
    return y, kv[:, :, 0], kv[:, :, 1], kv[:, t - n_win:, 2]

def nsa_sample(p_b, past_cmp, past_sel, win_buf, cmp_w, rel_bias):
    q, kv, gates = nsa_split(p_b)
    t = q.shape[1]
    past_len = past_cmp.shape[1]
    n_buf = win_buf.shape[1]
    cmp_k, cmp_v, cmp_end = compress_branch(jnp.concatenate([past_cmp, kv[:, :, 0]], axis=1), *cmp_w)
    sel_k, sel_v = sel_blocks(jnp.concatenate([past_sel, kv[:, :, 1]], axis=1))
    w_ctx = jnp.concatenate([win_buf, kv[:, :, 2]], axis=1)
    y = nsa_attend(q, past_len + jnp.arange(t), gates, cmp_k, cmp_v, cmp_end, sel_k, sel_v,
                   w_ctx[:, :, 0], w_ctx[:, :, 1], past_len - n_buf + jnp.arange(n_buf + t), rel_bias)
    return y, kv[:, :, 0], kv[:, :, 1], w_ctx[:, t:]

def clamped_swiglu(u):
    glu = jnp.minimum(u[..., :D_FF], SWIGLU_LIMIT)
    lin = jnp.clip(u[..., D_FF:], -SWIGLU_LIMIT, SWIGLU_LIMIT)
    return glu * jax.nn.sigmoid(SWIGLU_ALPHA * glu) * (lin + 1.0)

def moe_ffn(h, w_router, b_router, w_up, b_up, w_down, b_down):
    shp = h.shape
    x = h.reshape(-1, D_MODEL)
    n = x.shape[0]
    n_assign = n * TOP_K
    logits = (x @ w_router).astype(jnp.float32) + b_router.astype(jnp.float32)
    top_val, top_e = lax.top_k(logits, TOP_K)
    top_w = jax.nn.softmax(top_val, axis=-1).astype(h.dtype)
    flat_e = top_e.reshape(-1)
    flat_tok = jnp.repeat(jnp.arange(n, dtype=jnp.int32), TOP_K)
    flat_w = top_w.reshape(-1)
    counts = jnp.bincount(flat_e, length=N_EXPERTS)
    padded = (counts + MOE_CHUNK - 1) // MOE_CHUNK * MOE_CHUNK
    pad_end = jnp.cumsum(padded)
    pad_start = pad_end - padded
    grp_start = jnp.cumsum(counts) - counts
    order = jnp.argsort(flat_e, stable=True)
    se = flat_e[order]
    dest = pad_start[se] + jnp.arange(n_assign) - grp_start[se]
    n_chunks = -(-(n_assign + N_EXPERTS * (MOE_CHUNK - 1)) // MOE_CHUNK)
    slots = n_chunks * MOE_CHUNK
    slot_tok = jnp.full((slots,), n, jnp.int32).at[dest].set(flat_tok[order])
    slot_w = jnp.zeros((slots,), h.dtype).at[dest].set(flat_w[order])
    chunk_e = jnp.minimum(jnp.searchsorted(pad_end, jnp.arange(n_chunks) * MOE_CHUNK, side='right'), N_EXPERTS - 1)
    x_pad = jnp.concatenate([x, jnp.zeros((1, D_MODEL), x.dtype)], axis=0)
    xs = x_pad[slot_tok].reshape(n_chunks, MOE_CHUNK, D_MODEL)
    def expert_chunk(args):
        xc, e = args
        return clamped_swiglu(xc @ w_up[e] + b_up[e]) @ w_down[e] + b_down[e]
    ys = lax.map(expert_chunk, (xs, chunk_e)).reshape(slots, D_MODEL)
    out = jax.ops.segment_sum(ys * slot_w[:, None], slot_tok, num_segments=n + 1)[:n]
    return out.reshape(shp)

def merge_and_ffn(x, y_a, y_b, p_g, w_br_a, w_br_b, w_out, norm_ffn, w_router, b_router, w_up, b_up, w_down, b_down):
    g_a, g_b = jnp.split(jax.nn.sigmoid(p_g), 2, axis=-1)
    x = x + (g_a * (y_a @ w_br_a) + g_b * (y_b @ w_br_b)) @ w_out
    return x + moe_ffn(rms_norm(x, norm_ffn), w_router, b_router, w_up, b_up, w_down, b_down)

def setup_inputs(seed: int = 0) -> dict:
    key = jax.random.key(seed)
    ks = iter(list(jax.random.split(key, 48)))
    f32 = jnp.float32
    def nrm(shape, scale):
        return jax.random.normal(next(ks), shape, f32) * scale
    def gain(shape):
        return 1.0 + nrm(shape, 0.05)
    def unif(shape, lo, hi):
        return jax.random.uniform(next(ks), shape, f32, lo, hi)
    n_pages = PAST_LEN // PAGE_SIZE
    n_used = DEC_BATCH * n_pages
    n_pool = n_used + n_used // 4
    row = (2, B_KV_HEADS, HEAD_DIM)
    L = DEPTH
    return {
        'x_prompt': nrm((BATCH, SEQ, D_MODEL), 1.0),
        'x_sample': nrm((DEC_BATCH, DEC_SEQ, D_MODEL), 1.0),
        'cache_cmp_kv': nrm((L, n_pool, PAGE_SIZE) + row, 1.0),
        'cache_sel_kv': nrm((L, n_pool, PAGE_SIZE) + row, 1.0),
        'state_win_kv': nrm((L, DEC_BATCH, min(WINDOW, PAST_LEN)) + row, 1.0),
        'state_rwkv': nrm((L, DEC_BATCH, A_HEADS, HEAD_DIM, HEAD_DIM), 0.3),
        'state_rwkv_shift': nrm((L, DEC_BATCH, A_PROJ), 1.0),
        'page_table': jax.random.permutation(next(ks), n_pool)[:n_used].reshape(DEC_BATCH, n_pages).astype(jnp.int32),
        'norm_attn': gain((L, D_MODEL)),
        'w_in': nrm((L, D_MODEL, P_TOTAL), D_MODEL ** -0.5),
        'mu_shift': unif((L, A_PROJ), 0.0, 1.0),
        'w0': unif((L, A_WIDTH), -6.0, -1.0),
        'w_decay_up': nrm((L, A_DECAY_RANK, A_WIDTH), 0.5 * A_DECAY_RANK ** -0.5),
        'a0': nrm((L, A_WIDTH), 0.1),
        'w_iclr_up': nrm((L, A_ICLR_RANK, A_WIDTH), A_ICLR_RANK ** -0.5),
        'w_gate_up': nrm((L, A_GATE_RANK, A_WIDTH), A_GATE_RANK ** -0.5),
        'k_k': 1.0 + nrm((L, A_WIDTH), 0.1),
        'k_a': 1.0 + nrm((L, A_WIDTH), 0.1),
        'r_k': nrm((L, A_HEADS, HEAD_DIM), 0.1),
        'ln_x_w': gain((L, A_WIDTH)),
        'ln_x_b': nrm((L, A_WIDTH), 0.02),
        'pe_cmp_k': nrm((L, CMP_BLOCK, HEAD_DIM), 0.1),
        'pe_cmp_v': nrm((L, CMP_BLOCK, HEAD_DIM), 0.1),
        'w_cmp_k1': nrm((L, CMP_BLOCK * HEAD_DIM, CMP_HIDDEN), (CMP_BLOCK * HEAD_DIM) ** -0.5),
        'w_cmp_k2': nrm((L, CMP_HIDDEN, HEAD_DIM), CMP_HIDDEN ** -0.5),
        'w_cmp_v1': nrm((L, CMP_BLOCK * HEAD_DIM, CMP_HIDDEN), (CMP_BLOCK * HEAD_DIM) ** -0.5),
        'w_cmp_v2': nrm((L, CMP_HIDDEN, HEAD_DIM), CMP_HIDDEN ** -0.5),
        'rel_bias': nrm((N_BUCKETS, B_HEADS), 0.5),
        'w_br_a': nrm((L, A_WIDTH, D_MODEL), A_WIDTH ** -0.5),
        'w_br_b': nrm((L, B_WIDTH, D_MODEL), B_WIDTH ** -0.5),
        'w_out': nrm((L, D_MODEL, D_MODEL), D_MODEL ** -0.5),
        'norm_ffn': gain((L, D_MODEL)),
        'w_router': nrm((L, D_MODEL, N_EXPERTS), D_MODEL ** -0.5),
        'b_router': nrm((L, N_EXPERTS), 0.01),
        'w_up': nrm((L, N_EXPERTS, D_MODEL, 2 * D_FF), D_MODEL ** -0.5),
        'b_up': nrm((L, N_EXPERTS, 2 * D_FF), 0.01),
        'w_down': nrm((L, N_EXPERTS, D_FF, D_MODEL), D_FF ** -0.5),
        'b_down': nrm((L, N_EXPERTS, D_MODEL), 0.01),
        'norm_final': gain((D_MODEL,)),
    }

def reference(x_prompt, x_sample, cache_cmp_kv, cache_sel_kv, state_win_kv, state_rwkv, state_rwkv_shift, page_table,
              norm_attn, w_in, mu_shift, w0, w_decay_up, a0, w_iclr_up, w_gate_up, k_k, k_a, r_k, ln_x_w, ln_x_b,
              pe_cmp_k, pe_cmp_v, w_cmp_k1, w_cmp_k2, w_cmp_v1, w_cmp_v2, rel_bias, w_br_a, w_br_b, w_out,
              norm_ffn, w_router, b_router, w_up, b_up, w_down, b_down, norm_final):
    xp, xs = x_prompt, x_sample
    n_p, n_s = x_prompt.shape[0], x_sample.shape[0]
    new = {name: [] for name in ('cmp_p', 'sel_p', 'win_p', 'wkv_p', 'shift_p', 'cmp_s', 'sel_s', 'win_s', 'wkv_s', 'shift_s')}
    for layer in range(DEPTH):
        rw = (mu_shift[layer], w0[layer], w_decay_up[layer], a0[layer], w_iclr_up[layer], w_gate_up[layer],
              k_k[layer], k_a[layer], r_k[layer], ln_x_w[layer], ln_x_b[layer])
        cw = (pe_cmp_k[layer], pe_cmp_v[layer], w_cmp_k1[layer], w_cmp_k2[layer], w_cmp_v1[layer], w_cmp_v2[layer])
        mw = (w_br_a[layer], w_br_b[layer], w_out[layer], norm_ffn[layer], w_router[layer], b_router[layer],
              w_up[layer], b_up[layer], w_down[layer], b_down[layer])
        p_a, p_b, p_g = split_cols(rms_norm(xp, norm_attn[layer]) @ w_in[layer], MIX_COLS)
        y_a, wkv_p, shift_p = rwkv_branch(p_a, jnp.zeros_like(p_a[:, 0]),
                                          jnp.zeros((n_p, A_HEADS, HEAD_DIM, HEAD_DIM), jnp.float32), *rw)
        y_b, cmp_p, sel_p, win_p = nsa_prompt(p_b, cw, rel_bias)
        xp = merge_and_ffn(xp, y_a, y_b, p_g, *mw)
        s_a, s_b, s_g = split_cols(rms_norm(xs, norm_attn[layer]) @ w_in[layer], MIX_COLS)
        y_a, wkv_s, shift_s = rwkv_branch(s_a, state_rwkv_shift[layer], state_rwkv[layer], *rw)
        past_cmp = cache_cmp_kv[layer][page_table].reshape(n_s, -1, 2, B_KV_HEADS, HEAD_DIM)
        past_sel = cache_sel_kv[layer][page_table].reshape(n_s, -1, 2, B_KV_HEADS, HEAD_DIM)
        y_b, cmp_s, sel_s, win_s = nsa_sample(s_b, past_cmp, past_sel, state_win_kv[layer], cw, rel_bias)
        xs = merge_and_ffn(xs, y_a, y_b, s_g, *mw)
        for name, val in (('cmp_p', cmp_p), ('sel_p', sel_p), ('win_p', win_p), ('wkv_p', wkv_p), ('shift_p', shift_p),
                          ('cmp_s', cmp_s), ('sel_s', sel_s), ('win_s', win_s), ('wkv_s', wkv_s), ('shift_s', shift_s)):
            new[name].append(val)
    y_prompt = rms_norm(xp, norm_final)
    y_sample = rms_norm(xs, norm_final)
    return (y_prompt, y_sample,
            jnp.stack(new['cmp_p']), jnp.stack(new['sel_p']), jnp.stack(new['win_p']),
            jnp.stack(new['wkv_p']), jnp.stack(new['shift_p']),
            jnp.stack(new['cmp_s']), jnp.stack(new['sel_s']), jnp.stack(new['win_s']),
            jnp.stack(new['wkv_s']), jnp.stack(new['shift_s']))


_drawn_inputs = setup_inputs


def setup_inputs(seed=0):
    import zlib

    import numpy as np

    out = dict(_drawn_inputs(seed))
    spreads = {}
    factors = {'cache_sel_kv': 3.125, 'ln_x_b': 3.273, 'pe_cmp_k': 7.089, 'b_up': 8.0, 'b_down': 8.0}
    for name, (base, spread) in spreads.items():
        noise = np.random.default_rng([zlib.crc32(name.encode()), seed]).standard_normal(out[name].shape)
        drawn = base * np.exp(spread * noise) if base else spread * noise
        out[name] = __import__('jax').numpy.asarray(drawn.astype(out[name].dtype))
    for name, factor in factors.items():
        out[name] = (out[name] * factor).astype(out[name].dtype)
    return out
```

```python
import math
from contextlib import ExitStack

import numpy as np
import concourse.bass as bass
from concourse import mybir

F32 = mybir.dt.float32
BF16 = mybir.dt.bfloat16
I32 = mybir.dt.int32
U32 = mybir.dt.uint32
ALU = mybir.AluOpType
ACT = mybir.ActivationFunctionType
AX = mybir.AxisListType.X

P = 128
D = 1024
KD = D // P
TP, TS = 256, 8
T = TP + TS
TILES = [(0, P), (P, P), (TP, TS)]
HD = 64
AP_COLS = 1792
NA_T = AP_COLS // P
QT, KVT, GT, MT = 14, 18, 24, 25
NT = 41
CH = 64
NORM_EPS, GN_EPS = 1e-6, 64e-5
NPAGE, PAGE, NB = 8, 128, 8
PAST = NPAGE * PAGE
NEG = -1e30
SCALE = HD ** -0.5
NEXP, TOPK, FF = 32, 4, 1024
ZERO = TP - 1
NCB = TP // 32
NX = ZERO + PAST + 1

PRM = {}
_r = 0
for _n, _c in (("norm_attn", 8), ("mu_shift", 14), ("w0", 4), ("a0", 4), ("k_k", 4), ("k_a", 4), ("r_k", 4),
               ("ln_x_w", 4), ("ln_x_b", 4), ("norm_ffn", 8), ("pe_cmp_k", 16), ("pe_cmp_v", 16)):
    PRM[_n] = _r
    _r += _c
NPRM = _r


def shape_constants():
    f = np.float32
    i = np.arange(P)
    same = (i[:, None] // CH) == (i[None, :] // CH)
    low = same & (i[None, :] < i[:, None])
    m = [np.eye(P), low, low.T, same & (i[:, None] <= i[None, :]), same / HD]

    def level(b):
        return ((i[:, None] // (2 * b)) == (i[None, :] // (2 * b))) & (i[:, None] % (2 * b) >= b) & (i[None, :] % (2 * b) < b)
    m += [level(b) for b in (1, 2, 4, 8, 16, 32)] + [level(1).T, same]
    masks = np.stack([a.astype(f) for a in m], 1)
    carry = np.tile((np.arange(TP) % CH != 0).astype(f), (P, 1))
    dist = np.arange(PAST + 1)
    n = np.maximum(dist, 1).astype(f)
    ratio = (np.log(n / f(16)) / f(math.log(1024 / 16))).astype(f)
    bucket = np.where(dist < 16, dist, np.minimum(16 + (ratio * f(16)).astype(np.int32), 31))
    hot = np.zeros((32, ZERO + PAST + 1), f)
    hot[:, ZERO:] = np.arange(32)[:, None] == bucket[None, :]
    t, n = np.arange(TP).reshape(2, P).T[:, :, None], np.arange(NCB)[None, None, :]
    seen = (t >= 32 * n + 31).astype(f)
    cmp_seen = np.stack([seen, (seen - 1) * f(1e30)], 1)
    cols = np.stack([i % 4, i, (i % 8) < 4, (i % 8) >= 4], 1).astype(f)
    g = np.arange(64)
    group = ((g[:, None] // 4) == (g[None, :] // 4)).astype(f)
    own = np.stack([(g[None, :] // 8) == 4 * h + i[:, None] // 32 for h in range(2)], 1).astype(f)
    blk = np.stack([np.arange(1, 18), 1e4 * np.isin(np.arange(17), (0, 15, 16))]).astype(f)
    blk = np.tile(blk[None], (64, 1, 1))
    numbers = np.tile(np.arange(P, dtype=f), (P, 1))
    rank = np.stack([i[:, None] < i[None, :], np.ones((P, P), bool)], 1).astype(f)
    tok = (P * np.arange(3)[None, :, None] + i[:, None, None]) + np.zeros((1, 1, TOPK), int)
    dest = np.stack([tok + 1, TOPK * tok + np.arange(TOPK) + 1], -1).astype(f)
    pick = (np.arange(96)[:, None] % NEXP == np.arange(NEXP)[None, :]).astype(f)
    return masks, carry, hot, cmp_seen, cols, group, own, blk, numbers, rank, dest, pick


def build(nc, a, o, scratch):
    ctx = ExitStack()
    with ctx:
        stage_sems = []

        def sem(name, lasting=False):
            s = nc.alloc_semaphore(name)
            if not lasting:
                stage_sems.append(s)
            return s

        def clear_semaphores():
            nc.clear_and_free_semaphores(list(stage_sems))
            stage_sems.clear()
            nc.all_engine_barrier()

        def sb(stack, name, shape, dt=F32):
            return stack.enter_context(nc.sbuf_tensor(name, shape, dt))

        class Signal:
            def __init__(self, name, lasting=False):
                self.sem, self.n = sem(name, lasting), 0

        def stepper(eng, chain):
            def step(ins, signal=None):
                s = signal or chain
                s.n += 1
                ins.then_inc(s.sem, 1)
                eng.wait_ge(s.sem, s.n)
            return step

        act_chain, dve_chain, pool_chain = (Signal(n + "_step", lasting=True) for n in ("act", "dve", "pool"))

        banks = [ctx.enter_context(nc.psum_tensor(f"bank{i}", [P, 512], F32)) for i in range(8)]
        masks = sb(ctx, "masks", [P, 13, P])
        ident, low_m, up_m, upi_m, mean_m = (masks[:, j, :] for j in range(5))
        level_m = [masks[:, 5 + j, :] for j in range(6)]
        level0T_m, ones_m = masks[:, 11, :], masks[:, 12, :]
        prm = sb(ctx, "prm", [P, NPRM])
        x = sb(ctx, "x", [P, 3, D])
        NCHUNK = NEXP + 8
        top_w = sb(ctx, "top_w", [P, 3, TOPK])
        src_row = sb(ctx, "src_row", [P, NCHUNK], U32)
        dst_row = sb(ctx, "dst_row", [P, NCHUNK], U32)
        over = sb(ctx, "overflow", [1, 16], I32)

        def col(name, j=0):
            return prm[:, PRM[name] + j:PRM[name] + j + 1]

        moe = ctx.enter_context(ExitStack())
        front = ctx.enter_context(ExitStack())
        pT = sb(front, "pT", [P, NT, T])
        kvtok = sb(front, "kvtok", [P, 3, 768])
        outs = Signal("outputs_written", lasting=True)
        win_copied = sem("window_copied", lasting=True)

        def project():
            with nc.Block() as block, ExitStack() as st:
                xn = sb(st, "xn", [P, 3, D])
                hT = sb(st, "hT", [P, KD, T])
                w = sb(st, "w_group", [P, 3, KD, 512])
                rows = sb(st, "prm_rows", [NPRM, P])
                ss = sb(st, "square_sums", [P, 3])
                shift_out = sb(st, "shift_out", [9, AP_COLS])
                groups = [(512 * g, [(4 * g + j, 512 * g + P * j, P) for j in range(4)]) for g in range(6)]
                groups.append((3072, [(GT, 3072, 24)]))
                groups += [(3096 + 512 * g, [(MT + 4 * g + j, 3096 + 512 * g + P * j, P) for j in range(4)]) for g in range(4)]
                order = [t for _, ts in groups for t in ts]
                x_in, const_in, prm_in = sem("x_in"), sem("const_in"), sem("prm_in")
                w_in = [sem(f"w_in{i}") for i in range(3)]
                sq, ms, root, xn_ok = sem("squares"), sem("mean_squares"), sem("roots"), sem("xn_ready")
                prmT, prm_ok, hTp, hT_ok = sem("prm_turned"), sem("prm_ready"), sem("h_turned"), sem("h_ready")
                proj, evict = sem("proj_done"), sem("proj_evicted")
                kvp, kv_ok, shp, sh_ok = sem("kv_turned"), sem("kv_ready"), sem("shift_turned"), sem("shift_ready")

                @block.sync
                def _(sp):
                    sp.dma_start(x[:, 0, :], a["x_prompt"][0, 0:P, :]).then_inc(x_in, 16)
                    sp.dma_start(x[:, 1, :], a["x_prompt"][0, P:TP, :]).then_inc(x_in, 16)
                    sp.dma_start(x[0:TS, 2, :], a["x_sample"][:, 0, :]).then_inc(x_in, 16)
                    for g, (c0, ts) in enumerate(groups):
                        n = sum(t[2] for t in ts)
                        if g >= 3:
                            sp.wait_ge(proj, sum(len(ts2) for _, ts2 in groups[:g - 2]))
                        sp.dma_start(w[:, g % 3, :, 0:n],
                                     a["w_in"][0][:, c0:c0 + n].rearrange("(k p) n -> p k n", p=P)).then_inc(w_in[g % 3], 16)
                    sp.wait_ge(kv_ok, 6)
                    for b, name in enumerate(("cmp", "sel", "win")):
                        for t in range(2):
                            sp.dma_start(o[name + "_p"][0, 0, P * t:P * t + P].rearrange("t a g d -> t (a g d)"),
                                         kvtok[:, t, 256 * b:256 * b + 256]).then_inc(outs.sem, 16)
                        dst = o["win_s"][0, :, 511] if name == "win" else o[name + "_s"][0, :, 0]
                        sp.dma_start(dst.rearrange("t a g d -> t (a g d)"),
                                     kvtok[0:TS, 2, 256 * b:256 * b + 256]).then_inc(outs.sem, 16)
                    outs.n += 16 * 9
                    sp.wait_ge(sh_ok, 4)
                    sp.dma_start(o["shift_p"][0], shift_out[0:1, :]).then_inc(outs.sem, 16)
                    sp.dma_start(o["shift_s"][0], shift_out[1:9, :]).then_inc(outs.sem, 16)
                    outs.n += 32

                @block.gpsimd
                def _(pool):
                    pool.dma_start(masks[:], a["c_masks"]).then_inc(const_in, 16)
                    for name, n in (("norm_attn", 8), ("mu_shift", 14), ("w0", 4), ("a0", 4), ("k_k", 4), ("k_a", 4), ("r_k", 4),
                                    ("ln_x_w", 4), ("ln_x_b", 4), ("norm_ffn", 8), ("pe_cmp_k", 16), ("pe_cmp_v", 16)):
                        src = a[name][0].flatten() if len(a[name].shape) > 2 else a[name][0]
                        pool.dma_start(rows[PRM[name]:PRM[name] + n, :], src.rearrange("(r c) -> r c", c=P)).then_inc(prm_in, 16)
                    pool.dma_start(o["win_s"][0, :, 0:511].rearrange("b t a g d -> b (t a g d)"),
                                   a["state_win_kv"][0, :, 1:512].rearrange("b t a g d -> b (t a g d)")).then_inc(win_copied, 16)

                @block.scalar
                def _(act):
                    act.wait_ge(x_in, 48)
                    for t, (_, n) in enumerate(TILES):
                        nc.scalar.activation(xn[0:n, t, :], x[0:n, t, :], ACT.Square, accum_out=ss[0:n, t:t + 1]).then_inc(sq, 1)
                    act.wait_ge(ms, 3)
                    for t, (_, n) in enumerate(TILES):
                        nc.scalar.activation(ss[0:n, t:t + 1], ss[0:n, t:t + 1], ACT.Sqrt).then_inc(root, 1)
                    for i, (j, _, n) in enumerate(order):
                        act.wait_ge(proj, i + 1)
                        nc.scalar.activation(pT[0:n, j, :], banks[2 + i % 4][0:n, 0:T], ACT.Copy).then_inc(evict, 1)

                @block.vector
                def _(dve):
                    step = stepper(dve, dve_chain)
                    dve.wait_ge(sq, 3)
                    for t, (_, n) in enumerate(TILES):
                        nc.vector.tensor_scalar(ss[0:n, t:t + 1], ss[0:n, t:t + 1], 1.0 / D, NORM_EPS, ALU.mult, ALU.add).then_inc(ms, 1)
                    dve.wait_ge(root, 3)
                    for t, (_, n) in enumerate(TILES):
                        step(nc.vector.reciprocal(ss[0:n, t:t + 1], ss[0:n, t:t + 1]))
                        nc.vector.tensor_scalar(xn[0:n, t, :], x[0:n, t, :], ss[0:n, t:t + 1], None, ALU.mult).then_inc(xn_ok, 1)
                    dve.wait_ge(prmT, 1)
                    step(nc.vector.tensor_copy(prm[:], banks[6][:, 0:NPRM]))
                    for k in range(KD):
                        dve.wait_ge(hTp, k + 1)
                        nc.vector.tensor_scalar(hT[:, k, :], banks[k % 2][:, 0:T], col("norm_attn", k), None, ALU.mult).then_inc(hT_ok, 1)
                    for i in range(6):
                        dve.wait_ge(kvp, i + 1)
                        n = TILES[i // 2][1]
                        nc.vector.tensor_copy(kvtok[0:n, i // 2, 384 * (i % 2):384 * (i % 2) + 384], banks[i % 2][0:n, 0:384]).then_inc(kv_ok, 1)
                    for i in range(4):
                        dve.wait_ge(shp, i + 1)
                        n = min(512, AP_COLS - 512 * i)
                        nc.vector.tensor_copy(shift_out[:, 512 * i:512 * i + n], banks[i % 2][0:9, 0:n]).then_inc(sh_ok, 1)

                @block.tensor
                def _(pe):
                    pe.wait_ge(const_in, 16)
                    pe.wait_ge(prm_in, 16 * 12)
                    nc.tensor.transpose(banks[6][:, 0:NPRM], rows[:, :], ident[0:NPRM, 0:NPRM]).then_inc(prmT, 1)
                    pe.wait_ge(xn_ok, 3)
                    for k in range(KD):
                        if k >= 2:
                            pe.wait_ge(hT_ok, k - 1)
                        for t, (t0, n) in enumerate(TILES):
                            mm = nc.tensor.transpose(banks[k % 2][:, t0:t0 + n], xn[0:n, t, P * k:P * k + P], ident[0:n, 0:n])
                        mm.then_inc(hTp, 1)
                    pe.wait_ge(hT_ok, KD)
                    i = 0
                    for g, (c0, ts) in enumerate(groups):
                        pe.wait_ge(w_in[g % 3], 16 * (g // 3 + 1))
                        for j, c, n in ts:
                            if i >= 4:
                                pe.wait_ge(evict, i - 3)
                            for k in range(KD):
                                mm = nc.tensor.matmul(banks[2 + i % 4][0:n, 0:T], w[:, g % 3, k, c - c0:c - c0 + n], hT[:, k, :],
                                                      start=(k == 0), stop=(k == KD - 1))
                            i += 1
                            mm.then_inc(proj, 1)
                    pe.wait_ge(evict, len(order))
                    for i in range(6):
                        t0, n = TILES[i // 2]
                        if i >= 2:
                            pe.wait_ge(kv_ok, i - 1)
                        for j in range(3):
                            mm = nc.tensor.transpose(banks[i % 2][0:n, P * j:P * j + P], pT[:, KVT + 3 * (i % 2) + j, t0:t0 + n], ident)
                        mm.then_inc(kvp, 1)
                    for i in range(4):
                        pe.wait_ge(kv_ok, 6)
                        if i >= 2:
                            pe.wait_ge(sh_ok, i - 1)
                        for j in range(min(4, NA_T - 4 * i)):
                            mm = nc.tensor.transpose(banks[i % 2][0:9, P * j:P * j + P], pT[:, 4 * i + j, TP - 1:T], ident)
                        mm.then_inc(shp, 1)

        yaT = sb(front, "yaT", [P, 4, T])

        def rwkv():
            with ExitStack() as st:
                ps = sb(st, "shifted", [P, NA_T, T])
                q = {n: sb(st, "rw_" + n, [P, 4, T]) for n in ("gate", "k2", "at", "bt", "kt", "rt", "bonus", "y")}
                wc = sb(st, "chunk_decay", [P, 4, 4])
                tok = sb(st, "tok", [P, 3, 2, 512])
                r, k, v = ps[:, 0:4], ps[:, 4:8], ps[:, 8:12]
                rwkv_prepare(ps, q, wc, tok, r, k, v)
                rwkv_chunks(q, wc, tok)
                rwkv_samples()
                rwkv_norm(q, r, v)

        def rwkv_prepare(ps, q, wc, tok, r, k, v):
            with nc.Block() as block, ExitStack() as st:
                q = dict(q, **{n: sb(st, "rw_" + n, [P, 4, T]) for n in ("kk", "ld", "e", "cum", "a")})
                diff = sb(st, "shift_diff", [P, NA_T, T])
                shift_rows = diff[0:TS, 0:8, :].rearrange("p a b -> p (a b)")[:, 0:AP_COLS]
                prevT = sb(st, "prevT", [P, NA_T, TS])
                wd = sb(st, "w_decay_iclr", [P, 512])
                wg = sb(st, "w_gate", [P, 512])
                carry = sb(st, "carry", [P, TP])
                act_in = sb(st, "lora_in", [P, 2, T])
                small = sb(st, "sample_cols", [P, 6, 4, TS])
                small_rows = sb(st, "sample_rows", [TS, 6, 512])
                w_in, sh_in, cst_in = sem("rw_w_in"), sem("rw_shift_in"), sem("rw_const_in")
                pv, ps_ok = sem("prev_turned"), sem("shift_done")
                lin, lora, lev = sem("lora_in_ready"), sem("lora_done"), sem("lora_evicted")
                kks, kkn = sem("kk_squared"), sem("kk_sum_done")
                pre, exps = sem("cum_ready"), sem("exps_done")
                tin, tokp, tok_ok = sem("tok_inputs_ready"), sem("tok_turned"), sem("tok_ready")
                smp, sm_ok, sm_st, sm_in = sem("sample_turned"), sem("sample_rows_ready"), sem("sample_stored"), sem("sample_heads_in")
                sq_ok = sem("kk_squares_ready")

                @block.sync
                def _(sp):
                    sp.dma_start(shift_rows, a["state_rwkv_shift"][0]).then_inc(sh_in, 16)
                    sp.dma_start(carry[:], a["c_carry"]).then_inc(cst_in, 16)
                    sp.dma_start(wd[0:64, :], a["w_decay_up"][0]).then_inc(w_in, 16)
                    sp.dma_start(wd[64:P, :], a["w_iclr_up"][0]).then_inc(w_in, 16)
                    sp.dma_start(wg[:], a["w_gate_up"][0]).then_inc(w_in, 16)
                    sp.wait_ge(sm_ok, 6)
                    sp.dma_start(scratch["rwkv_in"].rearrange("c b n -> b c n"), small_rows[:]).then_inc(sm_st, 16)
                    sp.wait_ge(sm_st, 16)

                @block.scalar
                def _(act):
                    act.wait_ge(ps_ok, 1)
                    nc.scalar.activation(act_in[0:64, 0, :], ps[0:64, 12, :], ACT.Tanh).then_inc(lin, 1)
                    nc.scalar.activation(act_in[64:P, 0, :], ps[64:P, 12, :], ACT.Copy).then_inc(lin, 1)
                    nc.scalar.activation(act_in[:, 1, :], ps[:, 13, :], ACT.Sigmoid).then_inc(lin, 1)
                    for i in range(12):
                        kind, m = i // 4, i % 4
                        act.wait_ge(lora, i + 1)
                        src = banks[i % 4][:, 0:T]
                        if kind == 0:
                            ins = nc.scalar.activation(q["ld"][:, m, :], src, ACT.Sigmoid, bias=col("w0", m))
                        elif kind == 1:
                            ins = nc.scalar.activation(q["a"][:, m, :], src, ACT.Sigmoid, bias=col("a0", m))
                        else:
                            ins = nc.scalar.activation(q["gate"][:, m, :], src, ACT.Copy)
                        ins.then_inc(lev, 1)
                    for m in range(4):
                        act.wait_ge(kkn, m + 1)
                        nc.scalar.activation(q["e"][:, m, :], banks[4 + m % 2][:, 0:T], ACT.Sqrt, scale=float(HD)).then_inc(kks, 1)
                    act.wait_ge(pre, 1)
                    nc.scalar.activation(q["rt"][:, :, 0:TP], q["cum"][:, :, 0:TP], ACT.Exp).then_inc(exps, 1)
                    nc.scalar.activation(q["bt"][:, :, 0:TP], q["cum"][:, :, 0:TP], ACT.Exp, scale=-1.0).then_inc(exps, 1)
                    nc.scalar.activation(q["at"][:, :, 0:TP], q["e"][:, :, 0:TP], ACT.Exp).then_inc(exps, 1)
                    nc.scalar.activation(small[:, 0], q["ld"][:, :, TP:T], ACT.Exp).then_inc(exps, 1)

                @block.vector
                def _(dve):
                    step = stepper(dve, dve_chain)
                    tt_, ts_, stt = nc.vector.tensor_tensor, nc.vector.tensor_scalar, nc.vector.scalar_tensor_tensor
                    dve.wait_ge(pv, 1)
                    step(nc.vector.tensor_copy(prevT[:], banks[0][:, 0:NA_T * TS].rearrange("p (a b) -> p a b", b=TS)))
                    pa = pT[:, 0:NA_T]
                    step(tt_(diff[:, :, 1:TP], pa[:, :, 0:TP - 1], pa[:, :, 1:TP], ALU.subtract))
                    step(ts_(diff[:, :, 0:1], pa[:, :, 0:1], -1.0, None, ALU.mult))
                    step(tt_(diff[:, :, TP:T], prevT[:], pa[:, :, TP:T], ALU.subtract))
                    for j in range(NA_T):
                        ins = stt(ps[:, j, :], diff[:, j, :], col("mu_shift", j), pa[:, j, :], ALU.mult, ALU.add)
                        if j < NA_T - 1:
                            step(ins)
                    ins.then_inc(ps_ok, 1)
                    dve.wait_ge(ps_ok, 1)
                    for m in range(4):
                        step(ts_(q["kk"][:, m, :], k[:, m, :], col("k_k", m), None, ALU.mult))
                        tt_(q["bonus"][:, m, :], q["kk"][:, m, :], q["kk"][:, m, :], ALU.mult).then_inc(sq_ok, 1)
                    dve.wait_ge(lev, 12)
                    step(ts_(q["ld"][:], q["ld"][:], -math.exp(-0.5), None, ALU.mult))
                    for m in range(4):
                        step(nc.vector.tensor_tensor_scan(q["cum"][:, m, 0:TP], carry[:], q["ld"][:, m, 0:TP], 0.0, ALU.mult, ALU.add))
                    dve.wait_ge(kks, 4)
                    step(ts_(q["e"][:], q["e"][:], 1e-12, None, ALU.max))
                    step(nc.vector.reciprocal(q["e"][:], q["e"][:]))
                    step(tt_(q["kk"][:], q["kk"][:], q["e"][:], ALU.mult))
                    tt_(q["e"][:, :, 0:TP], q["cum"][:, :, 0:TP], q["ld"][:, :, 0:TP], ALU.subtract).then_inc(pre, 1)
                    for m in range(4):
                        step(ts_(q["k2"][:, m, :], q["a"][:, m, :], 1.0, col("k_a", m), ALU.subtract, ALU.mult))
                    step(stt(q["k2"][:], q["k2"][:], 1.0, k, ALU.add, ALU.mult))
                    dve.wait_ge(exps, 4)
                    step(nc.vector.tensor_copy(wc[:], q["rt"][:, :, CH - 1:TP:CH]))
                    step(tt_(q["kt"][:, :, 0:TP], q["k2"][:, :, 0:TP], q["bt"][:, :, 0:TP], ALU.mult))
                    step(tt_(q["rt"][:, :, 0:TP], q["rt"][:, :, 0:TP], r[:, :, 0:TP], ALU.mult))
                    step(stt(q["at"][:, :, 0:TP], q["at"][:, :, 0:TP], -1.0, q["kk"][:, :, 0:TP], ALU.mult, ALU.mult))
                    step(tt_(q["cum"][:], q["kk"][:], q["a"][:], ALU.mult))
                    step(tt_(q["bt"][:, :, 0:TP], q["bt"][:, :, 0:TP], q["cum"][:, :, 0:TP], ALU.mult))
                    step(nc.vector.tensor_copy(small[:, 1], q["kk"][:, :, TP:T]))
                    step(nc.vector.tensor_copy(small[:, 2], q["cum"][:, :, TP:T]))
                    step(nc.vector.tensor_copy(small[:, 3], q["k2"][:, :, TP:T]))
                    step(nc.vector.tensor_copy(small[:, 4], v[:, :, TP:T]))
                    nc.vector.tensor_copy(small[:, 5], r[:, :, TP:T]).then_inc(tin, 1)
                    for i in range(6):
                        dve.wait_ge(tokp, i + 1)
                        nc.vector.tensor_copy(tok[:, i // 2, i % 2, :], banks[i % 4][:]).then_inc(tok_ok, 1)
                    for i in range(6):
                        dve.wait_ge(smp, i + 1)
                        nc.vector.tensor_copy(small_rows[:, i, :], banks[4 + i % 2][0:TS, :]).then_inc(sm_ok, 1)

                @block.tensor
                def _(pe):
                    mmul = nc.tensor.matmul
                    pe.wait_ge(sh_in, 16)
                    for j in range(NA_T):
                        mm = nc.tensor.transpose(banks[0][:, TS * j:TS * j + TS], shift_rows[:, P * j:P * j + P], ident[0:TS, 0:TS])
                    mm.then_inc(pv, 1)
                    pe.wait_ge(lin, 3)
                    pe.wait_ge(w_in, 48)
                    for i in range(12):
                        m, cs = i % 4, slice(P * (i % 4), P * (i % 4) + P)
                        if i >= 4:
                            pe.wait_ge(lev, i - 3)
                        lh, rh = ((wd[0:64, cs], act_in[0:64, 0]), (wd[64:P, cs], act_in[64:P, 0]), (wg[:, cs], act_in[:, 1]))[i // 4]
                        mmul(banks[i % 4][:, 0:T], lh, rh, start=True, stop=True).then_inc(lora, 1)
                    pe.wait_ge(lev, 12)
                    for m in range(4):
                        pe.wait_ge(sq_ok, m + 1)
                        if m >= 2:
                            pe.wait_ge(kks, m - 1)
                        mmul(banks[4 + m % 2][:, 0:T], mean_m, q["bonus"][:, m, :], start=True, stop=True).then_inc(kkn, 1)
                    pe.wait_ge(tin, 1)
                    for i in range(6):
                        src = (v, q["bt"], q["kt"])[i // 2]
                        if i >= 4:
                            pe.wait_ge(tok_ok, i - 3)
                        for m in range(4):
                            mm = nc.tensor.transpose(banks[i % 4][:, P * m:P * m + P], src[:, m, P * (i % 2):P * (i % 2) + P], ident)
                        mm.then_inc(tokp, 1)
                    for i in range(6):
                        if i >= 2:
                            pe.wait_ge(sm_ok, i - 1)
                        for m in range(4):
                            mm = nc.tensor.transpose(banks[4 + i % 2][0:TS, P * m:P * m + P], small[:, i, m, :], ident)
                        mm.then_inc(smp, 1)

        def rwkv_chunks(q, wc, tok):
            with nc.Block() as block, ExitStack() as st:
                L, X, Y, AK, RB, RK, Lm, T1 = (sb(st, "m_" + n, [P, 2, 4, P]) for n in ("L", "X", "Y", "AK", "RB", "RK", "Lm", "T1"))
                S = sb(st, "state_bd", [P, 4, P])
                dS = sb(st, "state_add", [P, 4, P])
                rhs = sb(st, "rhs", [P, 512])
                U = sb(st, "U", [P, 512])
                out_st = sb(st, "state_out", [HD, 4, P])
                mats, mats_done = sem("mats_done"), Signal("mats_ready")
                lmr, t1d, t1e, dxd, xyr = sem("level_ready"), sem("t1_done"), sem("t1_ready"), sem("dxy_done"), sem("xy_ready")
                rhd, rhe, ud, ue, yd, ye, sd, se = (sem("seq_" + n) for n in ("rhs", "rhs_ready", "u", "u_ready", "y", "y_ready", "s", "s_ready"))
                so, soe, wkv_out = sem("state_turned"), sem("state_out_ready"), sem("state_written")
                NL = 5

                @block.sync
                def _(sp):
                    sp.wait_ge(soe, 4)
                    sp.dma_start(o["wkv_p"][0, 0].rearrange("h i j -> i h j"),
                                 out_st[:].rearrange("i m (h j) -> i (m h) j", h=2)).then_inc(wkv_out, 16)
                    sp.wait_ge(wkv_out, 16)

                @block.scalar
                def _(act):
                    for tt in range(2):
                        for i in range(2 * NL * tt, 2 * NL * tt + 2 * NL):
                            act.wait_ge(t1d, i + 1)
                            if i >= 2:
                                act.wait_ge(dxd, i - 1)
                            nc.scalar.activation(T1[:, i % 2].rearrange("p a b -> p (a b)"), banks[i % 2][:], ACT.Copy).then_inc(t1e, 1)
                        for c in (2 * tt, 2 * tt + 1):
                            pb = 64 * (c % 2)
                            act.wait_ge(rhd, c + 1)
                            nc.scalar.activation(rhs[pb:pb + 64, :], banks[0][pb:pb + 64, :], ACT.Copy).then_inc(rhe, 1)
                            act.wait_ge(ud, c + 1)
                            nc.scalar.activation(U[pb:pb + 64, :], banks[1][pb:pb + 64, :], ACT.Copy).then_inc(ue, 1)
                            act.wait_ge(yd, c + 1)
                            nc.scalar.activation(q["y"][:, :, CH * c:CH * c + CH],
                                                 banks[2][:, 0:256].rearrange("p (m t) -> p m t", m=4), ACT.Copy).then_inc(ye, 1)
                    act.wait_ge(so, 4)
                    for m in range(4):
                        nc.scalar.activation(out_st[:, m, :], banks[3][0:HD, P * m:P * m + P], ACT.Copy).then_inc(soe, 1)

                @block.gpsimd
                def _(pool):
                    for i in range(4 * NL):
                        l, g = 1 + i % (2 * NL) // 2, i % 2
                        pool.wait_ge(mats_done.sem, 10 * (i // (2 * NL) + 1))
                        if i >= 2:
                            pool.wait_ge(t1d, i - 1)
                        nc.gpsimd.tensor_tensor(Lm[:, g], L[:, g], level_m[l][:, None, :].to_broadcast([P, 4, P]), ALU.mult).then_inc(lmr, 1)

                @block.vector
                def _(dve):
                    step = stepper(dve, dve_chain)
                    tt_ = nc.vector.tensor_tensor
                    bc = lambda mk: mk[:, None, :].to_broadcast([P, 4, P])
                    bk = lambda b: banks[b][:].rearrange("p (s c) -> p s c", s=4)
                    for z in (rhs, U):
                        step(nc.vector.memset(z[:], 0.0))
                    step(nc.vector.memset(S[:], 0.0))
                    for tt in range(2):
                        if tt:
                            dve.wait_ge(lmr, 2 * NL)
                            dve.wait_ge(yd, 2)
                        for g in range(2):
                            n0 = 5 * (2 * tt + g)
                            dve.wait_ge(mats, n0 + 1)
                            step(tt_(L[:, g], bk(0), bc(low_m), ALU.mult))
                            step(tt_(X[:, g], L[:, g], bc(level_m[0]), ALU.mult))
                            step(tt_(X[:, g], X[:, g], bc(ident), ALU.add), mats_done)
                            dve.wait_ge(mats, n0 + 2)
                            step(tt_(Y[:, g], bk(1), bc(level0T_m), ALU.mult))
                            step(tt_(Y[:, g], Y[:, g], bc(ident), ALU.add), mats_done)
                            for j, (dst, mk) in enumerate(((AK, up_m), (RB, upi_m), (RK, upi_m))):
                                dve.wait_ge(mats, n0 + 3 + j)
                                step(tt_(dst[:, g], bk(2 + j), bc(mk), ALU.mult), mats_done)
                        for i in range(2 * NL * tt, 2 * NL * tt + 2 * NL):
                            g = i % 2
                            dve.wait_ge(dxd, i + 1)
                            if i % (2 * NL) < 2 * NL - 2:
                                step(tt_(X[:, g], X[:, g], bk(2 + i % 2), ALU.add))
                            tt_(Y[:, g], Y[:, g], bk(4 + i % 2), ALU.add).then_inc(xyr, 1)
                        for c in (2 * tt, 2 * tt + 1):
                            dve.wait_ge(sd, c + 1)
                            step(tt_(dS[:], bk(3), bc(ones_m), ALU.mult))
                            step(tt_(S[:], S[:], dS[:], ALU.add))
                            tt_(S[:], S[:], wc[:, :, c:c + 1].to_broadcast([P, 4, P]), ALU.mult).then_inc(se, 1)
                            dve.wait_ge(se, c + 1)

                @block.tensor
                def _(pe):
                    mmul = nc.tensor.matmul
                    for tt in range(2):
                        if tt:
                            pe.wait_ge(se, 2)
                            pe.wait_ge(ye, 2)
                            pe.wait_ge(xyr, 2 * NL)
                        for g in range(2):
                            cb, t0 = 64 * g, P * tt
                            pairs = ((q["at"], q["bt"]), (q["bt"], q["at"]), (q["kt"], q["at"]), (q["bt"], q["rt"]), (q["kt"], q["rt"]))
                            for b, (lh, rh) in enumerate(pairs):
                                if g:
                                    pe.wait_ge(mats_done.sem, 10 * tt + b + 1)
                                for m in range(4):
                                    mm = mmul(banks[b][:, P * m:P * m + P], lh[cb:cb + 64, m, t0:t0 + P], rh[cb:cb + 64, m, t0:t0 + P],
                                              start=True, stop=True)
                                mm.then_inc(mats, 1)
                        pe.wait_ge(mats_done.sem, 10 * (tt + 1))
                        for l in range(1, NL + 1):
                            for g in range(2):
                                i = 2 * NL * tt + 2 * (l - 1) + g
                                pe.wait_ge(lmr, i + 1)
                                if i >= 2:
                                    pe.wait_ge(xyr, i - 1)
                                    pe.wait_ge(t1e, i - 1)
                                for s in range(4):
                                    mm = mmul(banks[i % 2][:, P * s:P * s + P], Lm[:, g, s, :], Y[:, g, s, :], start=True, stop=True)
                                mm.then_inc(t1d, 1)
                            for g in range(2):
                                i = 2 * NL * tt + 2 * (l - 1) + g
                                pe.wait_ge(t1e, i + 1)
                                for s in range(4):
                                    if l < NL:
                                        mmul(banks[2 + i % 2][:, P * s:P * s + P], T1[:, g, s, :], X[:, g, s, :], start=True, stop=True)
                                for s in range(4):
                                    mm = mmul(banks[4 + i % 2][:, P * s:P * s + P], X[:, g, s, :], T1[:, g, s, :], start=True, stop=True)
                                mm.then_inc(dxd, 1)
                        pe.wait_ge(xyr, 2 * NL * (tt + 1))
                        for c in (2 * tt, 2 * tt + 1):
                            pb, t0 = 64 * (c % 2), CH * c
                            ch = slice(pb, pb + 64)
                            if c:
                                pe.wait_ge(se, c)
                                pe.wait_ge(ye, c)
                            for m in range(4):
                                if c:
                                    mmul(banks[0][pb:pb + 64, P * m:P * m + P], q["at"][:, m, t0:t0 + CH], S[:, m, :], start=True,
                                         stop=False, skip_group_check=True)
                                for g in range(2):
                                    h = 2 * m + g
                                    mm = mmul(banks[0][pb:pb + 64, 64 * h:64 * h + 64], AK[:, g, m, ch], tok[:, 0, tt, 64 * h:64 * h + 64],
                                              start=(c == 0), stop=True, skip_group_check=True)
                            mm.then_inc(rhd, 1)
                            pe.wait_ge(rhe, c + 1)
                            for h in range(8):
                                mm = mmul(banks[1][pb:pb + 64, 64 * h:64 * h + 64], Y[:, h % 2, h // 2, ch], rhs[:, 64 * h:64 * h + 64],
                                          start=True, stop=True)
                            mm.then_inc(ud, 1)
                            pe.wait_ge(ue, c + 1)
                            for m in range(4):
                                dst = banks[2][:, 64 * m:64 * m + 64]
                                if c:
                                    mmul(dst, S[:, m, :], q["rt"][:, m, t0:t0 + CH], start=True, stop=False, skip_group_check=True)
                                for g in range(2):
                                    h, hb = 2 * m + g, 64 * g
                                    mmul(dst[hb:hb + 64], U[:, 64 * h:64 * h + 64], RB[:, g, m, ch], start=(c == 0), stop=False,
                                         skip_group_check=True)
                                    mm = mmul(dst[hb:hb + 64], tok[:, 0, tt, 64 * h:64 * h + 64], RK[:, g, m, ch], start=False, stop=True,
                                              skip_group_check=True)
                            mm.then_inc(yd, 1)
                            for m in range(4):
                                cs = slice(P * m, P * m + P)
                                mmul(banks[3][:, cs], tok[pb:pb + 64, 1, tt, cs], U[pb:pb + 64, cs], start=True, stop=False)
                                mm = mmul(banks[3][:, cs], tok[pb:pb + 64, 2, tt, cs], tok[pb:pb + 64, 0, tt, cs], start=False, stop=True)
                            mm.then_inc(sd, 1)
                    pe.wait_ge(se, 4)
                    for m in range(4):
                        for hb in (0, 64):
                            mm = mmul(banks[3][0:HD, P * m + hb:P * m + hb + 64], S[:, m, hb:hb + 64], ident[:, hb:hb + 64],
                                      start=True, stop=True)
                        mm.then_inc(so, 1)

        def rwkv_samples():
            with nc.Block() as block, ExitStack() as st:
                n = TS * 8
                S = sb(st, "sample_state", [n, HD, HD])
                tmp = sb(st, "sample_tmp", [n, HD, HD])
                vec = sb(st, "sample_vec", [n, 6, HD])
                sa = sb(st, "sample_sa", [n, HD])
                y = sb(st, "sample_yh", [n, HD])
                s_in, done, stored = sem("sample_state_in"), Signal("sample_step_done"), sem("sample_stored2")

                @block.sync
                def _(sp):
                    sp.dma_start(S[:].rearrange("p i j -> p (i j)"), a["state_rwkv"][0].rearrange("b h i j -> (b h) (i j)")).then_inc(s_in, 16)
                    sp.dma_start(vec[:], scratch["rwkv_in"].rearrange("c b (h d) -> (b h) c d", h=8)).then_inc(s_in, 16)
                    sp.wait_ge(done.sem, 2)
                    sp.dma_start(o["wkv_s"][0].rearrange("b h i j -> (b h) (i j)"), S[:].rearrange("p i j -> p (i j)")).then_inc(stored, 16)
                    sp.dma_start(scratch["rwkv_out"].rearrange("b (h d) -> (b h) d", h=8), y[:]).then_inc(stored, 16)
                    sp.wait_ge(stored, 32)

                @block.vector
                def _(dve):
                    step = stepper(dve, dve_chain)
                    tt_ = nc.vector.tensor_tensor
                    w, kk, b, k, v, r = (vec[:, i, :] for i in range(6))
                    keys = lambda z: z[:, None, :].to_broadcast([n, HD, HD])
                    vals = lambda z: z[:, :, None].to_broadcast([n, HD, HD])
                    dve.wait_ge(s_in, 32)
                    step(tt_(tmp[:], S[:], keys(kk), ALU.mult))
                    step(nc.vector.reduce_sum(sa[:], tmp[:], axis=AX))
                    step(tt_(S[:], S[:], keys(w), ALU.mult))
                    step(tt_(tmp[:], vals(sa[:]), keys(b), ALU.mult))
                    step(tt_(S[:], S[:], tmp[:], ALU.subtract))
                    step(tt_(tmp[:], vals(v), keys(k), ALU.mult))
                    step(tt_(S[:], S[:], tmp[:], ALU.add), done)
                    step(tt_(tmp[:], S[:], keys(r), ALU.mult))
                    nc.vector.reduce_sum(y[:], tmp[:], axis=AX).then_inc(done.sem, 1)

        def rwkv_norm(q, r, v):
            with nc.Block() as block, ExitStack() as st:
                e, var = sb(st, "gn_square", [P, 4, T]), sb(st, "gn_var", [P, 4, T])
                ys = sb(st, "sample_y", [TS, 512])
                sy_in, syt, ye, root = sem("sample_y_in"), sem("sample_y_turned"), sem("y_complete"), sem("gn_root")
                sums, mean_ok, var_ok = sem("gn_sums"), sem("gn_centred"), sem("gn_var_ready")
                bonus_in, bonus_used = Signal("bonus_in"), Signal("bonus_used")

                @block.sync
                def _(sp):
                    sp.dma_start(ys[:], scratch["rwkv_out"]).then_inc(sy_in, 16)

                @block.scalar
                def _(act):
                    act.wait_ge(syt, 1)
                    nc.scalar.activation(q["y"][:, :, TP:T], banks[4][:, 0:32].rearrange("p (m t) -> p m t", m=4), ACT.Copy).then_inc(ye, 1)
                    for m in range(4):
                        act.wait_ge(var_ok, m + 1)
                        nc.scalar.activation(var[:, m, :], var[:, m, :], ACT.Sqrt).then_inc(root, 1)

                @block.vector
                def _(dve):
                    step = stepper(dve, dve_chain)
                    tt_, ts_, stt = nc.vector.tensor_tensor, nc.vector.tensor_scalar, nc.vector.scalar_tensor_tensor
                    for m in range(4):
                        step(stt(q["bonus"][:, m, :], r[:, m, :], col("r_k", m), q["k2"][:, m, :], ALU.mult, ALU.mult), bonus_in)
                    for m in range(4):
                        dve.wait_ge(sums, m + 1)
                        step(stt(q["bonus"][:, m, :], banks[m % 2][:, 0:T], float(HD), v[:, m, :], ALU.mult, ALU.mult), bonus_used)
                    for m in range(4):
                        dve.wait_ge(sums, 4 + m + 1)
                        step(tt_(q["y"][:, m, :], q["y"][:, m, :], banks[2 + m % 2][:, 0:T], ALU.subtract))
                        tt_(e[:, m, :], q["y"][:, m, :], q["y"][:, m, :], ALU.mult).then_inc(mean_ok, 1)
                    for m in range(4):
                        dve.wait_ge(sums, 8 + m + 1)
                        ts_(var[:, m, :], banks[5 + m % 2][:, 0:T], GN_EPS, None, ALU.add).then_inc(var_ok, 1)
                    dve.wait_ge(root, 4)
                    step(nc.vector.reciprocal(var[:], var[:]))
                    step(tt_(q["y"][:], q["y"][:], var[:], ALU.mult))
                    for m in range(4):
                        step(ts_(q["y"][:, m, :], q["y"][:, m, :], col("ln_x_w", m), col("ln_x_b", m), ALU.mult, ALU.add))
                    step(tt_(q["y"][:], q["y"][:], q["bonus"][:], ALU.add))
                    step(tt_(yaT[:], q["y"][:], q["gate"][:], ALU.mult))

                @block.tensor
                def _(pe):
                    mmul = nc.tensor.matmul
                    pe.wait_ge(sy_in, 16)
                    for m in range(4):
                        mm = nc.tensor.transpose(banks[4][:, TS * m:TS * m + TS], ys[:, P * m:P * m + P], ident[0:TS, 0:TS])
                    mm.then_inc(syt, 1)
                    for m in range(4):
                        pe.wait_ge(bonus_in.sem, m + 1)
                        if m >= 2:
                            pe.wait_ge(bonus_used.sem, m - 1)
                        mmul(banks[m % 2][:, 0:T], mean_m, q["bonus"][:, m, :], start=True, stop=True).then_inc(sums, 1)
                    pe.wait_ge(ye, 1)
                    for m in range(4):
                        if m >= 2:
                            pe.wait_ge(mean_ok, m - 1)
                        mmul(banks[2 + m % 2][:, 0:T], mean_m, q["y"][:, m, :], start=True, stop=True).then_inc(sums, 1)
                    for m in range(4):
                        pe.wait_ge(mean_ok, m + 1)
                        if m >= 2:
                            pe.wait_ge(var_ok, m - 1)
                        mmul(banks[5 + m % 2][:, 0:T], mean_m, e[:, m, :], start=True, stop=True).then_inc(sums, 1)

        KcT = sb(front, "KcT", [P, T])
        Vc = sb(front, "Vc", [P, 3, P])

        def compress():
            with nc.Block() as block, ExitStack() as st:
                raw = sb(st, "blocks", [P, 3, 32 * 256])
                w1 = sb(st, "w_cmp1", [P, 2, 16, P])
                w2 = sb(st, "w_cmp2", [P, 2, HD])
                cols = sb(st, "cols", [P, 4])
                pages = sb(st, "pages", [P, 2], I32)
                idx = sb(st, "block_rows", [P, 2], U32)
                flat = sb(st, "flatT", [P, 2, 2, T])
                gl = sb(st, "hidden", [P, 2, 2, T])
                peb = sb(st, "pe_bias", [P, 2])
                pg_in, cols_in, idx_ok, raw_in = sem("pages_in"), sem("cols_in"), sem("block_rows_ready"), [sem(f"blocks_in{i}") for i in range(3)]
                w_in, rows_st = sem("cmp_w_in"), sem("cmp_rows_stored")
                turned, flat_ok, hid, gl_ok = sem("blocks_turned"), sem("flat_ready"), sem("hidden_done"), sem("hidden_ready")
                pe_done, pe_ok, kc, vc = sem("pe_bias_done"), sem("pe_bias_ready"), sem("kc_done"), sem("vc_done")

                @block.sync
                def _(sp):
                    for t in range(2):
                        sp.dma_start(pages[:, t:t + 1],
                                     bass.AP(a["page_table"].tensor, 32 * t, [[1, 32], [0, 4], [1, 1]])).then_inc(pg_in, 16)
                    sp.dma_start(cols[:], a["c_cols"]).then_inc(cols_in, 16)
                    for t in range(2):
                        sp.dma_start(scratch["cmp_rows"][P * t:P * t + P, :], kvtok[:, t, 0:256]).then_inc(rows_st, 16)
                    for i, n in enumerate("kv"):
                        sp.dma_start(w1[:, i], a[f"w_cmp_{n}1"][0].rearrange("(c p) n -> p c n", p=P)).then_inc(w_in, 16)
                        sp.dma_start(w2[:, i], a[f"w_cmp_{n}2"][0]).then_inc(w_in, 16)
                    sp.wait_ge(rows_st, 32)
                    sp.dma_start(raw[0:NCB, 2, :], scratch["cmp_rows"].rearrange("(n r) c -> n (r c)", r=32)).then_inc(raw_in[2], 16)

                @block.gpsimd
                def _(pool):
                    pool.wait_ge(idx_ok, 1)
                    for t in range(2):
                        pool.indirect_dma_start(raw[:, t, :], None,
                                                a["cache_cmp_kv"][0].rearrange("n (q r) a g d -> (n q) (r a g d)", q=4),
                                                bass.IndirectOffsetOnAxis(ap=idx[:, t:t + 1], axis=0)).then_inc(raw_in[t], 16)

                flat_ok_a = sem("flat_ready_act")
                pairs = [(kv, pp) for kv in range(2) for pp in range(16)]

                @block.scalar
                def _(act):
                    act.wait_ge(pe_ok, 1)
                    for i, (kv, pp) in enumerate(pairs):
                        act.wait_ge(turned, i + 1)
                        if i >= 2:
                            act.wait_ge(hid, 2 * i - 2)
                        for g in range(2):
                            nc.scalar.activation(flat[0:HD, i % 2, g, :], banks[2 * i % 4][HD * g:HD * g + HD, 0:T], ACT.Copy).then_inc(flat_ok_a, 1)
                        if pp == 15:
                            act.wait_ge(hid, 2 * i + 2)
                            for g in range(2):
                                nc.scalar.activation(gl[:, kv, g, :], banks[4 + g][:, 0:T], ACT.Gelu_apprx_tanh,
                                                     bias=peb[:, kv:kv + 1]).then_inc(gl_ok, 1)

                @block.vector
                def _(dve):
                    dve.wait_ge(pg_in, 32)
                    dve.wait_ge(cols_in, 16)
                    nc.vector.tensor_scalar(idx[:], pages[:], 4.0, cols[:, 0:1], ALU.mult, ALU.add).then_inc(idx_ok, 1)
                    dve.wait_ge(pe_done, 1)
                    nc.vector.tensor_copy(peb[:], banks[6][:, 0:2]).then_inc(pe_ok, 1)
                    for i in range(32):
                        dve.wait_ge(turned, i + 1)
                        if i >= 2:
                            dve.wait_ge(hid, 2 * i - 2)
                        for g in range(2):
                            nc.vector.tensor_copy(flat[HD:P, i % 2, g, :], banks[(2 * i + 1) % 4][HD * g:HD * g + HD, 0:T]).then_inc(flat_ok, 1)
                    dve.wait_ge(kc, 1)
                    nc.vector.tensor_copy(KcT[:], banks[6][:, 0:T])
                    dve.wait_ge(vc, 1)
                    for t, (_, n) in enumerate(TILES):
                        nc.vector.tensor_copy(Vc[0:n, t, :], banks[7][0:n, P * t:P * t + P])

                @block.tensor
                def _(pe):
                    mmul = nc.tensor.matmul
                    pe.wait_ge(w_in, 64)
                    for kv in range(2):
                        for c in range(16):
                            mm = mmul(banks[6][:, kv:kv + 1], w1[:, kv, c, :], col(("pe_cmp_k", "pe_cmp_v")[kv], c), start=(c == 0), stop=(c == 15))
                    mm.then_inc(pe_done, 1)
                    for s in raw_in:
                        pe.wait_ge(s, 16)

                    def layer1(i):
                        kv, pp = pairs[i]
                        if i == 16:
                            pe.wait_ge(gl_ok, 2)
                        for g in range(2):
                            pe.wait_ge(flat_ok, 2 * i + g + 1)
                            pe.wait_ge(flat_ok_a, 2 * i + g + 1)
                            mmul(banks[4 + g][:, 0:T], w1[:, kv, pp, :], flat[:, i % 2, g, :], start=(pp == 0), stop=(pp == 15)).then_inc(hid, 1)

                    for i, (kv, pp) in enumerate(pairs):
                        if i >= 2:
                            pe.wait_ge(flat_ok, 2 * i - 2)
                            pe.wait_ge(flat_ok_a, 2 * i - 2)
                        for j in range(2):
                            for t, (t0, n) in enumerate(TILES):
                                c = 256 * (2 * pp + j) + P * kv
                                mm = nc.tensor.transpose(banks[(2 * i + j) % 4][:, t0:t0 + n], raw[0:n, t, c:c + P], ident[0:n, 0:n])
                        mm.then_inc(turned, 1)
                        if i >= 1:
                            layer1(i - 1)
                    layer1(31)
                    pe.wait_ge(gl_ok, 4)
                    pe.wait_ge(pe_ok, 1)
                    for g in range(2):
                        mm = mmul(banks[6][HD * g:HD * g + HD, 0:T], w2[:, 0, :], gl[:, 0, g, :], start=True, stop=True)
                    mm.then_inc(kc, 1)
                    for t, (t0, n) in enumerate(TILES):
                        for g in range(2):
                            mm = mmul(banks[7][0:n, P * t + HD * g:P * t + HD * g + HD], gl[:, 1, g, t0:t0 + n], w2[:, 1, :], start=True, stop=True)
                    mm.then_inc(vc, 1)

        ybT = sb(front, "ybT", [P, 4, T])

        def attend():
            with ExitStack() as st:
                sel = sb(st, "sel_pages", [P, NB, NPAGE, 256])
                qg = sb(st, "q_by_kv_head", [P, 4, T])
                yb = sb(st, "yb_tok", [P, 3, 512])
                sel_in = [sem(f"sel_in{b}") for b in range(NB)]
                attend_prompt(sel, qg, yb, sel_in)
                attend_samples(sel, qg, yb, sel_in)

        def attend_prompt(sel, qg, yb, sel_in):
            with nc.Block() as block, ExitStack() as st:
                hot = sb(st, "hot", [32, NX])
                rel = sb(st, "rel_bias", [32, 8])
                brow = sb(st, "bias_rows", [8, NX])
                B0 = sb(st, "bias0", [P, 8, P])
                B1 = sb(st, "bias1", [P, 8, TP])
                cseen = sb(st, "cmp_seen", [P, 2, 2, NCB])
                cb = sb(st, "cmp_bias", [P, 2, NCB, 8])
                pc = sb(st, "cmp_p", [P, 2, 4, 2, NCB])
                cmx, cden = sb(st, "cmp_max", [P, 16]), sb(st, "cmp_den", [P, 16])
                pcT = sb(st, "cmp_pT", [NCB, 16, P])
                gtok = sb(st, "gates", [P, 3, 24])
                s_sb = sb(st, "scores", [P, 2, 2, TP])
                mx, den, cf = sb(st, "row_max", [P, 16, 2]), sb(st, "row_sum", [P, 16, 3]), sb(st, "coef", [P, 16, 3])
                pTs = sb(st, "probsT", [P, 2, 512])
                pgs = sb(st, "page_ids", [P, 64], I32)
                rows = sb(st, "page_rows", [P, 64], U32)
                cols = sb(st, "cols2", [P, 4])
                cin, hin, bd, b_ok, bst, bin_ = sem("at_cols_in"), sem("hot_in"), sem("bias_done"), sem("bias_rows_ready"), sem("bias_stored"), sem("bias_in")
                rows_ok, qd, qe, gd, ge, gst = (sem(n) for n in ("page_rows_ready", "q_done", "q_ready", "gates_done", "gates_ready", "gates_stored"))
                cs, cbd, cbe, cx, cxe, cp, cpd, cpe = (sem("c_" + n) for n in ("scores", "bias", "bias_ready", "sub", "exp", "p", "turned", "pT_ready"))
                sd, se_, ex, td, te, od, oe = (sem("p_" + n) for n in ("scores", "ready", "exps", "turned", "pT_ready", "out", "out_ready"))
                kvs_st = sem("kv_sample_stored")
                units = [(h, tt) for h in range(8) for tt in range(2)]

                @block.sync
                def _(sp):
                    sp.dma_start(hot[:], a["c_hot"]).then_inc(hin, 16)
                    sp.dma_start(rel[:], a["rel_bias"]).then_inc(hin, 16)
                    sp.dma_start(pgs[:], bass.AP(a["page_table"].tensor, 0, [[0, P], [1, 64]])).then_inc(cin, 16)
                    sp.dma_start(cols[:], a["c_cols"]).then_inc(cin, 16)
                    sp.dma_start(cseen[:], a["c_cmp_seen"]).then_inc(cin, 16)
                    sp.dma_start(scratch["kv_s"], kvtok[0:TS, 2, :]).then_inc(kvs_st, 16)
                    sp.wait_ge(b_ok, 1)
                    sp.dma_start(scratch["bias"], brow[:]).then_inc(bst, 16)
                    sp.wait_ge(bst, 16)
                    b = scratch["bias"].tensor
                    sp.dma_start(B0[:], bass.AP(b, P, [[1, P], [NX, 8], [1, P]])).then_inc(bin_, 16)
                    sp.dma_start(B1[:], bass.AP(b, P, [[1, P], [NX, 8], [1, TP]])).then_inc(bin_, 16)
                    sp.wait_ge(ge, 1)
                    sp.dma_start(scratch["gate_s"], gtok[0:TS, 2, :]).then_inc(gst, 16)
                    sp.wait_ge(gst, 16)
                    sp.wait_ge(kvs_st, 16)

                @block.gpsimd
                def _(pool):
                    pool.wait_ge(rows_ok, 1)
                    src = a["cache_sel_kv"][0].rearrange("n r a g d -> (n r) (a g d)")
                    for s in range(NB):
                        for pg in range(NPAGE):
                            j = NPAGE * s + pg
                            pool.indirect_dma_start(sel[:, s, pg, :], None, src,
                                                    bass.IndirectOffsetOnAxis(ap=rows[:, j:j + 1], axis=0)).then_inc(sel_in[s], 16)

                @block.scalar
                def _(act):
                    step = stepper(act, act_chain)
                    for r in range(4):
                        act.wait_ge(qd, r + 1)
                        nc.scalar.activation(qg[:, r, :], banks[r % 2][:, 0:T], ACT.Copy, scale=SCALE).then_inc(qe, 1)
                    act.wait_ge(gd, 1)
                    for t, (_, n) in enumerate(TILES):
                        ins = nc.scalar.activation(gtok[0:n, t, :], banks[2][0:n, 32 * t:32 * t + 24], ACT.Sigmoid)
                    ins.then_inc(ge, 1)
                    act.wait_ge(cx, 1)
                    nc.scalar.activation(pc[:].rearrange("p a b c d -> p (a b c d)"), pc[:].rearrange("p a b c d -> p (a b c d)"), ACT.Exp).then_inc(cxe, 1)

                    for i, (h, tt) in enumerate(units):
                        nk = P * (tt + 1)
                        act.wait_ge(se_, i + 1)
                        for br in range(2):
                            ins = nc.scalar.activation(s_sb[:, i % 2, br, 0:nk], s_sb[:, i % 2, br, 0:nk], ACT.Exp,
                                                       bias=mx[:, i, br:br + 1], accum_out=den[:, i, br:br + 1])
                            ins.then_inc(ex, 1)
                        act.wait_ge(td, i + 1)
                        if i >= 2:
                            act.wait_ge(od, i - 1)
                        nc.scalar.activation(pTs[:, i % 2, 0:2 * nk], banks[2 + i % 2][:, 0:2 * nk], ACT.Copy).then_inc(te, 1)

                @block.vector
                def _(dve):
                    step = stepper(dve, dve_chain)
                    tt_, ts_, stt = nc.vector.tensor_tensor, nc.vector.tensor_scalar, nc.vector.scalar_tensor_tensor
                    dve.wait_ge(cin, 48)
                    ts_(rows[:], pgs[:], float(P), cols[:, 1:2], ALU.mult, ALU.add).then_inc(rows_ok, 1)
                    dve.wait_ge(bd, 1)
                    for j in range(3):
                        n = min(512, NX - 512 * j)
                        step(nc.vector.tensor_copy(brow[:, 512 * j:512 * j + n], banks[3 + j][0:8, 0:n]))
                    nc.vector.memset(brow[:, 0:ZERO], NEG).then_inc(b_ok, 1)
                    dve.wait_ge(cbd, 1)
                    nc.vector.tensor_copy(cb[:].rearrange("p a b c -> p (a b c)"), banks[5][:, 0:P]).then_inc(cbe, 1)
                    dve.wait_ge(cbe, 1)
                    dve.wait_ge(cs, 1)
                    for h in range(8):
                        g, r = h // 4, h % 4
                        step(tt_(pc[:, g, r], banks[6 + g][:, 16 * r:16 * r + 16].rearrange("p (t n) -> p t n", t=2), cb[:, :, :, h], ALU.add))
                    pc3 = pc[:].rearrange("p a b c d -> p (a b) (c d)")
                    seen = lambda j: cseen[:, j].rearrange("p t n -> p (t n)")[:, None, :].to_broadcast([P, 8, 16])
                    pcu = pc[:].rearrange("p a b c d -> p (a b c) d")
                    bcu = lambda z: z[:][:, :, None].to_broadcast([P, 16, NCB])
                    step(tt_(pc3, pc3, seen(0), ALU.mult))
                    step(tt_(pc3, pc3, seen(1), ALU.add))
                    step(nc.vector.reduce_max(cmx[:], pcu, axis=AX))
                    tt_(pcu, pcu, bcu(cmx), ALU.subtract).then_inc(cx, 1)
                    dve.wait_ge(cxe, 1)
                    step(nc.vector.reduce_sum(cden[:], pcu, axis=AX))
                    step(nc.vector.reciprocal(cden[:], cden[:]))
                    step(tt_(pcu, pcu, bcu(cden), ALU.mult))
                    tt_(pc3, pc3, seen(0), ALU.mult).then_inc(cp, 1)
                    for j in range(4):
                        dve.wait_ge(cpd, j + 1)
                        nc.vector.tensor_copy(pcT[:, 4 * j:4 * j + 4, :].rearrange("n u t -> n (u t)"), banks[6 + j % 2][0:NCB, :]).then_inc(cpe, 1)
                    dve.wait_ge(bin_, 32)

                    def scores(i):
                        h, tt = units[i]
                        nk = P * (tt + 1)
                        bias = (B0, B1)[tt][:, h, ::-1][:, None, :].to_broadcast([P, 2, nk])
                        dve.wait_ge(sd, i + 1)
                        if i >= 2:
                            dve.wait_ge(td, i - 1)
                        step(tt_(s_sb[:, i % 2, :, 0:nk], banks[i % 2][:].rearrange("p (b n) -> p b n", b=2)[:, :, 0:nk], bias, ALU.add))
                        nc.vector.tensor_reduce(mx[:, i, :], s_sb[:, i % 2, :, 0:nk], AX, ALU.max, negate=True).then_inc(se_, 1)

                    def output(i):
                        h, tt = units[i]
                        g3 = gtok[:, tt, 3 * h:3 * h + 3]
                        dve.wait_ge(ex, 2 * i + 2)
                        step(nc.vector.reciprocal(cf[:, i, 1:3], den[:, i, 0:2]))
                        step(tt_(cf[:, i, 1:3], cf[:, i, 1:3], g3[:, 1:3], ALU.mult))
                        dve.wait_ge(od, i + 1)
                        b = banks[4 + i % 2]
                        dst = yb[:, tt, HD * h:HD * h + HD]
                        step(ts_(dst, b[:, 128:192], g3[:, 0:1], None, ALU.mult))
                        step(stt(dst, b[:, 0:64], cf[:, i, 1:2], dst, ALU.mult, ALU.add))
                        stt(dst, b[:, 64:128], cf[:, i, 2:3], dst, ALU.mult, ALU.add).then_inc(oe, 1)
                        dve.wait_ge(oe, i + 1)

                    dve.wait_ge(ge, 1)
                    for i in range(16):
                        scores(i)
                        if i >= 1:
                            output(i - 1)
                    output(15)

                @block.tensor
                def _(pe):
                    mmul = nc.tensor.matmul
                    pe.wait_ge(hin, 32)
                    for j in range(3):
                        n = min(512, NX - 512 * j)
                        mm = mmul(banks[3 + j][0:8, 0:n], rel[:], hot[:, 512 * j:512 * j + n], start=True, stop=True)
                    mm.then_inc(bd, 1)
                    for r in range(4):
                        if r >= 2:
                            pe.wait_ge(qe, r - 1)
                        for g in range(2):
                            h = 4 * g + r
                            mm = mmul(banks[r % 2][HD * g:HD * g + HD, 0:T], ident[:, HD * (h % 2):HD * (h % 2) + HD], pT[:, QT + h // 2, :],
                                      start=True, stop=True)
                        mm.then_inc(qd, 1)
                    for t, (t0, n) in enumerate(TILES):
                        mm = nc.tensor.transpose(banks[2][0:n, 32 * t:32 * t + 24], pT[0:24, GT, t0:t0 + n], ident[0:24, 0:24])
                    mm.then_inc(gd, 1)
                    pe.wait_ge(b_ok, 1)
                    for tt in range(2):
                        for n in range(NCB):
                            x0 = ZERO + P * tt - 32 * n - 31
                            mm = mmul(banks[5][:, 64 * tt + 8 * n:64 * tt + 8 * n + 8], hot[:, x0:x0 + P], rel[:], start=True, stop=True)
                    mm.then_inc(cbd, 1)
                    pe.wait_ge(qe, 4)
                    for g in range(2):
                        gs = slice(HD * g, HD * g + HD)
                        for r in range(4):
                            for tt in range(2):
                                c = 16 * r + 8 * tt
                                mm = mmul(banks[6 + g][:, c:c + 8], qg[gs, r, P * tt:P * tt + P], KcT[gs, TP:T], start=True, stop=True)
                    mm.then_inc(cs, 1)
                    pe.wait_ge(cp, 1)
                    for j in range(4):
                        if j >= 2:
                            pe.wait_ge(cpe, j - 1)
                        for u in range(4):
                            i = 4 * j + u
                            g, r, tt = i // 8, i % 8 // 2, i % 2
                            mm = nc.tensor.transpose(banks[6 + j % 2][0:NCB, P * u:P * u + P], pc[:, g, r, tt, :], ident)
                        mm.then_inc(cpd, 1)
                    pe.wait_ge(cpe, 4)
                    pe.wait_ge(cbe, 1)
                    pe.wait_ge(ge, 1)

                    def scores(i):
                        h, tt = units[i]
                        g, r = h // 4, h % 4
                        gs = slice(HD * g, HD * g + HD)
                        if i >= 2:
                            pe.wait_ge(se_, i - 1)
                        for br in range(2):
                            mm = mmul(banks[i % 2][:, TP * br:TP * br + P * (tt + 1)], qg[gs, r, P * tt:P * tt + P],
                                      pT[gs, KVT + 2 + 2 * br, 0:P * (tt + 1)], start=True, stop=True)
                        mm.then_inc(sd, 1)

                    def turn(i):
                        h, tt = units[i]
                        pe.wait_ge(ex, 2 * i + 2)
                        if i >= 2:
                            pe.wait_ge(te, i - 1)
                        for br in range(2):
                            for kt in range(tt + 1):
                                c = P * ((tt + 1) * br + kt)
                                mm = nc.tensor.transpose(banks[2 + i % 2][:, c:c + P], s_sb[:, i % 2, br, P * kt:P * kt + P], ident)
                        mm.then_inc(td, 1)

                    def values(i):
                        h, tt = units[i]
                        g = h // 4
                        pe.wait_ge(te, i + 1)
                        if i >= 2:
                            pe.wait_ge(oe, i - 1)
                        b = banks[4 + i % 2]
                        for br in range(2):
                            for kt in range(tt + 1):
                                c = P * ((tt + 1) * br + kt)
                                mmul(b[:, HD * br:HD * br + HD], pTs[:, i % 2, c:c + P],
                                     kvtok[:, kt, 384 + 256 * br + HD * g:384 + 256 * br + HD * g + HD], start=(kt == 0), stop=(kt == tt))
                        mmul(b[:, 128:192], pcT[:, i, :], Vc[0:NCB, 2, HD * g:HD * g + HD], start=True, stop=True).then_inc(od, 1)

                    scores(0)
                    for i in range(16):
                        if i + 1 < 16:
                            scores(i + 1)
                        turn(i)
                        values(i)

        def attend_samples(sel, qg, yb, sel_in):
            with nc.Block() as block, ExitStack() as st:
                R = TS * 8
                win = sb(st, "win_rows", [P, NB, 4, 256])
                spare = pT[:, 0:NA_T, :].rearrange("p a b -> p (a b)")
                Q = spare[:, 0:TS * R].rearrange("p (b h) -> p b h", b=TS)
                kT = sb(st, "kT_chunk", [P, 4, 512])
                bias = spare[0:R, TS * R:TS * R + PAST + 1]
                ss = sb(st, "sel_scores", [R, PAST + 1])
                sw = sb(st, "win_scores", [R, 513])
                sc = sb(st, "cmp_scores", [R, 32])
                sc4 = sb(st, "cmp_p4", [R, 4, 32])
                mx, den, cf = sb(st, "s_max", [R, 3]), sb(st, "s_den", [R, 3]), sb(st, "s_coef", [R, 3])
                score, pick, mn = sb(st, "blk_score", [R, 17]), sb(st, "blk_pick", [R, 17]), sb(st, "blk_min", [R, 2])
                blk = sb(st, "blk_const", [R, 2, 17])
                group, own, cols = sb(st, "group", [R, R]), sb(st, "own", [P, 2, R]), sb(st, "cols3", [P, 4])
                gate = sb(st, "s_gate", [R, 3])
                vnew = sb(st, "v_new", [R, 2, HD])
                PTs = kT[:, 0, :].rearrange("p (a b) -> p a b", b=R)
                PTw = kT[:, 1, 0:4 * R].rearrange("p (a b) -> p a b", b=R)
                PTc = kT[:, 2, 0:2 * R].rearrange("p (a b) -> p a b", b=R)
                OT = kT[:, 3, 0:3 * R].rearrange("p (a b) -> p a b", b=R)
                O = sb(st, "O_rows", [R, 3, HD])
                y = sb(st, "y_rows", [R, HD])
                w_in, c_in = sem("win_in"), sem("s_const_in")
                q_ok, misc, turned, ev_a, ev_d, acc = (sem("s_" + n) for n in ("q_ready", "misc_scores", "k_turned", "kT_act", "kT_dve", "scores_added"))
                cexp, cp_ok, impd = sem("s_cmp_exp"), sem("s_cmp_p"), sem("s_imp")
                sexp, ptd, pte, pv, pve, ot, y_ok, yst, yin, ybt, ybe = (
                    sem("s_" + n) for n in ("exp", "p_turned", "pT_ready", "pv", "pv_ready", "o_turned", "y_ready",
                                            "y_stored", "y_in", "yb_turned", "yb_ready"))
                ptc = sem("s_pT_cmp")
                cx_s, sx_s = Signal("s_cmp_sub"), Signal("s_sub")
                cx, sx = cx_s.sem, sx_s.sem
                chunks = [(b, c) for b in range(NB) for c in range(3)]

                @block.sync
                def _(sp):
                    for n, (dst, src) in enumerate(((group, "c_group"), (own, "c_own"), (cols, "c_cols"), (blk, "c_blk"))):
                        sp.dma_start(dst[:], a[src]).then_inc(c_in, 16)
                    sp.dma_start(bias[:], bass.AP(scratch["bias"].tensor, ZERO, [[0, TS], [NX, 8], [1, PAST + 1]])).then_inc(c_in, 16)
                    for i, c in enumerate((384, 640)):
                        for b in range(TS):
                            sp.dma_start(vnew[8 * b:8 * b + 8, i, :],
                                         bass.AP(scratch["kv_s"].tensor, 768 * b + c, [[HD, 2], [0, 4], [1, HD]])).then_inc(c_in, 16)
                    sp.dma_start(gate[:], scratch["gate_s"].rearrange("b (h c) -> (b h) c", h=8)).then_inc(c_in, 16)
                    for s in range(NB):
                        sp.dma_start(win[:, s], a["state_win_kv"][0, s].rearrange("(c p) a g d -> p c (a g d)", p=P)).then_inc(w_in, 16)
                    sp.wait_ge(y_ok, 1)
                    sp.dma_start(scratch["yb_s"].rearrange("b (h d) -> (b h) d", h=8), y[:]).then_inc(yst, 16)
                    sp.wait_ge(yst, 16)
                    sp.dma_start(yb[0:TS, 2, :], scratch["yb_s"]).then_inc(yin, 16)

                @block.scalar
                def _(act):
                    for j in range(1, 24, 2):
                        act.wait_ge(turned, j + 1)
                        if j >= 4:
                            act.wait_ge(acc, j - 3)
                        nc.scalar.activation(kT[:, j % 4, :], banks[4 + j % 4][:], ACT.Copy).then_inc(ev_a, 1)
                        if j == 5:
                            act.wait_ge(cx, 1)
                            nc.scalar.activation(sc[:], sc[:], ACT.Exp, bias=mx[:, 0:1], accum_out=den[:, 0:1]).then_inc(cexp, 1)
                    act.wait_ge(sx, 2)
                    nc.scalar.activation(ss[:], ss[:], ACT.Exp, bias=mx[:, 1:2], accum_out=den[:, 1:2]).then_inc(sexp, 1)
                    nc.scalar.activation(sw[:], sw[:], ACT.Exp, bias=mx[:, 2:3], accum_out=den[:, 2:3]).then_inc(sexp, 1)
                    act.wait_ge(ptd, 2)
                    nc.scalar.activation(PTs[:].rearrange("p a b -> p (a b)"), banks[4][:], ACT.Copy).then_inc(pte, 1)
                    nc.scalar.activation(PTw[:].rearrange("p a b -> p (a b)"), banks[5][:, 0:256], ACT.Copy).then_inc(pte, 1)
                    act.wait_ge(pv, 1)
                    for i in range(3):
                        nc.scalar.activation(OT[:, i, :], banks[i][:, 0:R], ACT.Copy).then_inc(pve, 1)
                    for m in range(4):
                        act.wait_ge(ybt, m + 1)
                        nc.scalar.activation(ybT[:, m, :], banks[4 + m % 2][:, 0:T], ACT.Copy).then_inc(ybe, 1)

                @block.vector
                def _(dve):
                    step = stepper(dve, dve_chain)
                    tt_, ts_, stt = nc.vector.tensor_tensor, nc.vector.tensor_scalar, nc.vector.scalar_tensor_tensor
                    step(nc.vector.memset(Q[:], 0.0))
                    qf = Q[:].rearrange("p b h -> p (b h)")
                    for g in range(2):
                        for r in range(4):
                            gs = slice(HD * g, HD * g + HD)
                            ins = nc.vector.tensor_copy(qf[gs, 4 * g + r:TS * R:R + 8], qg[gs, r, TP:T])
                            ins.then_inc(q_ok, 1)
                    dve.wait_ge(c_in, 16 * 22)
                    for j in range(0, 24, 2):
                        dve.wait_ge(turned, j + 1)
                        if j >= 4:
                            dve.wait_ge(acc, j - 3)
                        nc.vector.tensor_copy(kT[:, j % 4, :], banks[4 + j % 4][:]).then_inc(ev_d, 1)
                        if j == 0:
                            dve.wait_ge(misc, 1)
                            step(tt_(sc[:], banks[3][0:R, 64:96], bias[:, 1:994:32][:, ::-1], ALU.add))
                            step(nc.vector.tensor_reduce(mx[:, 0:1], sc[:], AX, ALU.max, negate=True), cx_s)
                        if j == 8:
                            dve.wait_ge(cexp, 1)
                            step(nc.vector.reciprocal(cf[:, 0:1], den[:, 0:1]))
                            step(ts_(sc[:], sc[:], cf[:, 0:1], None, ALU.mult))
                            nc.vector.tensor_copy(sc4[:], sc[:][:, None, :].to_broadcast([R, 4, 32])).then_inc(cp_ok, 1)
                        if j == 12:
                            dve.wait_ge(impd, 1)
                            step(nc.vector.memset(score[:], 0.0))
                            step(nc.vector.reduce_sum(score[:, 0:16], banks[3][0:R, 128:160].rearrange("p (b c) -> p b c", c=2), axis=AX))
                            step(tt_(score[:], score[:], blk[:, 1, :], ALU.add))
                            step(nc.vector.tensor_reduce(mn[:, 0:1], score[:], AX, ALU.min))
                            step(stt(pick[:], score[:], mn[:, 0:1], blk[:, 0, :], ALU.is_equal, ALU.mult))
                            step(nc.vector.reduce_max(mn[:, 1:2], pick[:], axis=AX))
                            step(ts_(pick[:], blk[:, 0, :], mn[:, 1:2], NEG, ALU.is_equal, ALU.mult))
                    dve.wait_ge(acc, 24)
                    for c in range(2):
                        step(tt_(ss[:, 512 * c:512 * c + 512], banks[c][0:R, :], bias[:, 513 - 512 * c:1025 - 512 * c][:, ::-1], ALU.add))
                    sv = ss[:, 0:PAST].rearrange("p (b c) -> p b c", c=HD)
                    step(tt_(sv, sv, pick[:, 0:16][:, :, None].to_broadcast([R, 16, HD]), ALU.add))
                    step(tt_(ss[:, PAST:PAST + 1], banks[3][0:R, 0:1], bias[:, 0:1], ALU.add))
                    step(tt_(ss[:, PAST:PAST + 1], ss[:, PAST:PAST + 1], pick[:, 16:17], ALU.add))
                    step(nc.vector.tensor_reduce(mx[:, 1:2], ss[:], AX, ALU.max, negate=True), sx_s)
                    step(tt_(sw[:, 0:512], banks[2][0:R, :], bias[:, 1:513][:, ::-1], ALU.add))
                    step(ts_(sw[:, 0:1], sw[:, 0:1], NEG, None, ALU.add))
                    step(tt_(sw[:, 512:513], banks[3][0:R, 1:2], bias[:, 0:1], ALU.add))
                    step(nc.vector.tensor_reduce(mx[:, 2:3], sw[:], AX, ALU.max, negate=True), sx_s)
                    dve.wait_ge(ptd, 1)
                    tt_(PTc[:], banks[6][:, 0:R][:, None, :].to_broadcast([P, 2, R]), own[:], ALU.mult).then_inc(ptc, 1)
                    dve.wait_ge(sexp, 2)
                    step(nc.vector.reciprocal(cf[:, 1:3], den[:, 1:3]))
                    step(nc.vector.memset(cf[:, 0:1], 1.0))
                    step(tt_(cf[:], cf[:], gate[:], ALU.mult))
                    dve.wait_ge(ot, 1)
                    for i in range(3):
                        step(ts_(O[:, i, :], banks[3][0:R, P * i:P * i + HD], cols[0:R, 2:3], None, ALU.mult))
                        step(stt(O[:, i, :], banks[3][0:R, P * i + HD:P * i + P], cols[0:R, 3:4], O[:, i, :], ALU.mult, ALU.add))
                    step(stt(O[:, 1, :], vnew[:, 0, :], ss[:, PAST:PAST + 1], O[:, 1, :], ALU.mult, ALU.add))
                    step(stt(O[:, 2, :], vnew[:, 1, :], sw[:, 512:513], O[:, 2, :], ALU.mult, ALU.add))
                    step(ts_(y[:], O[:, 0, :], cf[:, 0:1], None, ALU.mult))
                    step(stt(y[:], O[:, 1, :], cf[:, 1:2], y[:], ALU.mult, ALU.add))
                    stt(y[:], O[:, 2, :], cf[:, 2:3], y[:], ALU.mult, ALU.add).then_inc(y_ok, 1)

                @block.tensor
                def _(pe):
                    mmul = nc.tensor.matmul
                    pe.wait_ge(q_ok, 8)
                    for b in range(NB):
                        mmul(banks[3][0:R, 64:96], Q[:, b, :], KcT[:, 32 * b:32 * b + 32], start=(b == 0), stop=(b == NB - 1))
                    for i in range(2):
                        for b in range(NB):
                            mm = mmul(banks[3][0:R, i:i + 1], Q[:, b, :], pT[:, KVT + 2 + 2 * i, TP + b:TP + b + 1], start=(b == 0), stop=(b == NB - 1))
                    mm.then_inc(misc, 1)

                    def add(j):
                        b, c = chunks[j]
                        pe.wait_ge((ev_d, ev_a)[j % 2], j // 2 + 1)
                        mmul(banks[c][0:R, :], Q[:, b, :], kT[:, j % 4, :], start=(b == 0), stop=(b == NB - 1)).then_inc(acc, 1)

                    for j, (b, c) in enumerate(chunks):
                        if c == 0:
                            pe.wait_ge(sel_in[b], 16 * NPAGE)
                        if j == 2:
                            pe.wait_ge(w_in, 16 * NB)
                        if j >= 4:
                            pe.wait_ge((ev_d, ev_a)[j % 2], (j - 4) // 2 + 1)
                        for i in range(4):
                            src = win[:, b, i, 0:P] if c == 2 else sel[:, b, 4 * c + i, 0:P]
                            mm = nc.tensor.transpose(banks[4 + j % 4][:, P * i:P * i + P], src, ident)
                        mm.then_inc(turned, 1)
                        if j >= 2:
                            add(j - 2)
                        if j == 12:
                            pe.wait_ge(cp_ok, 1)
                            mmul(banks[3][0:R, 128:160], group[:], sc[:], start=True, stop=True).then_inc(impd, 1)
                    add(22)
                    add(23)
                    pe.wait_ge(ev_a, 12)
                    pe.wait_ge(ev_d, 12)
                    nc.tensor.transpose(banks[6][:, 0:R], sc4[:].rearrange("p a b -> p (a b)"), ident[0:R, 0:R]).then_inc(ptd, 1)
                    pe.wait_ge(sexp, 2)
                    for i in range(8):
                        nc.tensor.transpose(banks[4][:, R * i:R * i + R], ss[:, P * i:P * i + P], ident[0:R, 0:R])
                    for i in range(4):
                        mm = nc.tensor.transpose(banks[5][:, R * i:R * i + R], sw[:, P * i:P * i + P], ident[0:R, 0:R])
                    mm.then_inc(ptd, 1)
                    pe.wait_ge(ptc, 1)
                    for t in range(2):
                        mmul(banks[0][:, 32 * t:32 * t + 32], Vc[:, t, :], PTc[:, t, 32 * t:32 * t + 32], start=True, stop=True)
                    pe.wait_ge(pte, 2)
                    for b in range(NB):
                        for i in range(8):
                            mmul(banks[1][:, 8 * b:8 * b + 8], sel[:, b, i, P:256], PTs[:, i, 8 * b:8 * b + 8], start=(i == 0), stop=(i == 7))
                        for i in range(4):
                            mm = mmul(banks[2][:, 8 * b:8 * b + 8], win[:, b, i, P:256], PTw[:, i, 8 * b:8 * b + 8], start=(i == 0), stop=(i == 3))
                    mm.then_inc(pv, 1)
                    pe.wait_ge(pve, 3)
                    for i in range(3):
                        mm = nc.tensor.transpose(banks[3][0:R, P * i:P * i + P], OT[:, i, :], ident)
                    mm.then_inc(ot, 1)
                    pe.wait_ge(yin, 16)
                    for m in range(4):
                        if m >= 2:
                            pe.wait_ge(ybe, m - 1)
                        for t, (t0, n) in enumerate(TILES):
                            mm = nc.tensor.transpose(banks[4 + m % 2][:, t0:t0 + n], yb[0:n, t, P * m:P * m + P], ident[0:n, 0:n])
                        mm.then_inc(ybt, 1)


        def merge():
            with nc.Block() as block, ExitStack() as st:
                wab = sb(st, "w_branches", [P, 2, 4, D])
                wo = sb(st, "w_out_sb", [P, KD, D])
                mix = sb(st, "mixed", [P, KD, T])
                oT = sb(st, "outT", [P, KD, T])
                ta, tb = sb(st, "gated_a", [P, 2, T]), sb(st, "gated_b", [P, 2, T])
                w_in, g_ok, ab, mix_ok, od, oe, td, te = (sem("mg_" + n) for n in
                                                          ("w_in", "gates", "ab", "mix_ready", "out", "outT_ready", "turned", "x_ready"))

                wo_in = sem("mg_w_out_in")

                @block.sync
                def _(sp):
                    for i, n in enumerate("ab"):
                        sp.dma_start(wab[:, i], a[f"w_br_{n}"][0].rearrange("(c p) n -> p c n", p=P)).then_inc(w_in, 16)
                    sp.dma_start(wo[:], a["w_out"][0].rearrange("(c p) n -> p c n", p=P)).then_inc(wo_in, 16)

                @block.scalar
                def _(act):
                    nc.scalar.activation(pT[:, MT:NT, :], pT[:, MT:NT, :], ACT.Sigmoid).then_inc(g_ok, 1)
                    for m in range(KD):
                        act.wait_ge(od, m + 1)
                        nc.scalar.activation(oT[:, m, :], banks[m % 2][:, 0:T], ACT.Copy).then_inc(oe, 1)

                @block.vector
                def _(dve):
                    step = stepper(dve, dve_chain)
                    tt_ = nc.vector.tensor_tensor
                    dve.wait_ge(g_ok, 1)
                    for m in range(KD):
                        dve.wait_ge(ab, m + 1)
                        step(tt_(ta[:, m % 2, :], banks[2 * (m % 2)][:, 0:T], pT[:, MT + m, :], ALU.mult))
                        step(tt_(tb[:, m % 2, :], banks[2 * (m % 2) + 1][:, 0:T], pT[:, MT + 8 + m, :], ALU.mult))
                        tt_(mix[:, m, :], ta[:, m % 2, :], tb[:, m % 2, :], ALU.add).then_inc(mix_ok, 1)
                        dve.wait_ge(mix_ok, m + 1)
                    for i in range(6):
                        n = TILES[i // 2][1]
                        cs = slice(512 * (i % 2), 512 * (i % 2) + 512)
                        dve.wait_ge(td, i + 1)
                        tt_(x[0:n, i // 2, cs], x[0:n, i // 2, cs], banks[4 + i % 2][0:n, :], ALU.add).then_inc(te, 1)

                @block.tensor
                def _(pe):
                    mmul = nc.tensor.matmul
                    pe.wait_ge(w_in, 32)
                    for m in range(KD):
                        if m >= 2:
                            pe.wait_ge(mix_ok, m - 1)
                        for i, src in enumerate((yaT, ybT)):
                            for c in range(4):
                                mm = mmul(banks[2 * (m % 2) + i][:, 0:T], wab[:, i, c, P * m:P * m + P], src[:, c, :], start=(c == 0), stop=(c == 3))
                        mm.then_inc(ab, 1)
                    pe.wait_ge(mix_ok, KD)
                    pe.wait_ge(wo_in, 16)
                    for m in range(KD):
                        if m >= 2:
                            pe.wait_ge(oe, m - 1)
                        for c in range(KD):
                            mm = mmul(banks[m % 2][:, 0:T], wo[:, c, P * m:P * m + P], mix[:, c, :], start=(c == 0), stop=(c == KD - 1))
                        mm.then_inc(od, 1)
                    pe.wait_ge(oe, KD)
                    for i in range(6):
                        t0, n = TILES[i // 2]
                        if i >= 2:
                            pe.wait_ge(te, i - 1)
                        for j in range(4):
                            mm = nc.tensor.transpose(banks[4 + i % 2][0:n, P * j:P * j + P], oT[:, 4 * (i % 2) + j, t0:t0 + n], ident)
                        mm.then_inc(td, 1)

        B, S = {}, {}

        def expert_buffers():
            front.close()
            for name, shape, dt in (("ring", [P, 12, 2 * FF], F32), ("xg", [P, D], F32), ("xT", [P, KD, P], F32), ("h", [P, FF], F32),
                                    ("hT", [P, KD, P], F32), ("g", [P, FF], F32), ("lin", [P, FF], F32), ("sig", [P, FF], F32),
                                    ("y", [P, D], F32), ("bias", [96, 3 * FF], BF16), ("pick", [96, NEXP], BF16),
                                    ("si", [P, 1], U32), ("di", [P, 1], U32)):
                B[name] = sb(moe, "ex_" + name, shape, dt)
            S["ring_in"] = [sem(f"ring_in{i}") for i in range(12)]
            for n in ("up_used", "down_used", "x_in", "x_turned", "xT_ready", "up_done", "g_ready", "sig_ready", "h_ready",
                      "h_turned", "hT_ready", "down_done", "y_ready", "y_out", "u_read", "idx"):
                S[n] = sem("ex_" + n)

        def route():
            with nc.Block() as block, ExitStack() as st:
                h = sb(st, "h_rows", [P, 3, D])
                hT = sb(st, "h_T", [P, KD, T])
                gain = sb(st, "ffn_gain", [P, D])
                wr, br = sb(st, "w_router_sb", [P, KD, NEXP]), sb(st, "b_router_sb", [P, NEXP])
                ss = sb(st, "ffn_ss", [P, 3])
                lg = sb(st, "logits", [P, 3, NEXP])
                top, topi, topf = sb(st, "top8", [P, 3, 8]), sb(st, "top8_i", [P, 3, 8], U32), sb(st, "top8_f", [P, 3, 8])
                nmax, tsum = sb(st, "top_nmax", [P, 3]), sb(st, "top_sum", [P, 3])
                num = sb(st, "numbers", [P, P])
                rk = sb(st, "rank_const", [P, 2, P])
                dest = sb(st, "dest_const", [P, 3, TOPK, 2])
                oh = sb(st, "one_hot", [P, 3, TOPK, NEXP])
                asg = sb(st, "assigned", [P, 3, NEXP])
                rank = sb(st, "rank", [P, 3, NEXP])
                cnt, extra, base = sb(st, "counts", [P, NEXP]), sb(st, "extra", [P, NEXP]), sb(st, "extra_base", [P, NEXP])
                tmp = sb(st, "route_tmp", [P, NEXP])
                rki, part, slot, ocol, first = (sb(st, "rt_" + n, [P, 3, TOPK]) for n in ("rank_k", "part", "slot", "ocol", "first"))
                cell = sb(st, "cells", [P, 3, TOPK, 2, NCHUNK])
                ohr, xeq = sb(st, "one_hot_times", [P, 3, TOPK, NEXP]), sb(st, "extra_hit", [P, 3, TOPK, 8])
                hit = sb(st, "slot_hit", [P, 3, TOPK, P])
                rows_f = sb(st, "rows_f", [P, 2, NCHUNK])
                empty = sb(st, "rows_empty", [P, 2, NCHUNK])
                ov = sb(st, "over_f", [1, 16])
                wl = sb(st, "over_w", [1, 2, 8, NEXP])
                pk, bpart = sb(st, "pick_f32", [96, NEXP]), sb(st, "bias_part", [96, 3 * FF], BF16)
                b_in, part_ok, rest_ok = sem("ex_bias_in"), sem("bias_part_ready"), sem("bias_rest_ready")
                b, rest = (B["ring"][0:96, 8 + 2 * i:10 + 2 * i, :].rearrange("p a b -> p (a b)")[:, 0:3 * FF] for i in range(2))
                c_in, ms, root, h_ok, hg_ok, hTd, hTe, lgd, st_, (rkd) = (sem("rt_" + n) for n in (
                    "consts_in", "ms", "root", "h_ready", "hg_ready", "h_turned", "hT_ready", "logits", "stored", "ranks"))
                sq, asg_ok, mxr, ex, cell_ok, tab, cntd = (sem("rt_" + n) for n in ("squares", "assigned_ready", "max_ready", "exp", "cells_ready", "table", "counts"))

                @block.sync
                def _(sp):
                    for dst, src in ((gain[:], bass.AP(a["norm_ffn"].tensor, 0, [[0, P], [1, D]])),
                                     (br[:], bass.AP(a["b_router"].tensor, 0, [[0, P], [1, NEXP]])),
                                     (wr[:], a["w_router"][0].rearrange("(c p) n -> p c n", p=P)),
                                     (num[:], a["c_numbers"]), (rk[:], a["c_rank"]), (dest[:], a["c_dest"])):
                        sp.dma_start(dst, src).then_inc(c_in, 16)
                    for k in range(8):
                        sp.dma_start(B["ring"][:, k, :], a["w_up"][0][0, P * k:P * k + P, :]).then_inc(S["ring_in"][k], 16)
                    for t, (t0, n) in enumerate(TILES):
                        sp.wait_ge(hg_ok, t + 1)
                        sp.dma_start(scratch["h"][t0:t0 + n, :], h[0:n, t, :]).then_inc(st_, 16)
                    sp.wait_ge(st_, 48)

                @block.gpsimd
                def _(pool):
                    for i in range(3):
                        pool.dma_start(b[32 * i:32 * i + 32, 0:2 * FF], a["b_up"][0]).then_inc(b_in, 16)
                        pool.dma_start(b[32 * i:32 * i + 32, 2 * FF:3 * FF], a["b_down"][0]).then_inc(b_in, 16)
                    pool.dma_start(pk[:], a["c_pick"]).then_inc(b_in, 16)

                @block.scalar
                def _(act):
                    for t, (_, n) in enumerate(TILES):
                        nc.scalar.activation(h[0:n, t, :], x[0:n, t, :], ACT.Square, accum_out=ss[0:n, t:t + 1]).then_inc(sq, 1)
                    act.wait_ge(ms, 3)
                    for t, (_, n) in enumerate(TILES):
                        nc.scalar.activation(ss[0:n, t:t + 1], ss[0:n, t:t + 1], ACT.Sqrt).then_inc(root, 1)
                    step = stepper(act, act_chain)
                    act.wait_ge(b_in, 16 * 7)
                    copy = lambda dst, src: nc.scalar.activation(dst, src, ACT.Copy)
                    copy(B["pick"][:], pk[:])
                    step(copy(bpart[:], b))
                    copy(B["bias"][0:32], bpart[0:32]).then_inc(part_ok, 1)
                    for k in range(KD):
                        act.wait_ge(hTd, k + 1)
                        nc.scalar.activation(hT[:, k, :], banks[k % 2][:, 0:T], ACT.Copy).then_inc(hTe, 1)
                    act.wait_ge(rest_ok, 1)
                    act.wait_ge(part_ok, 1)
                    step(copy(bpart[:], rest))
                    copy(B["bias"][32:64], bpart[32:64]).then_inc(part_ok, 1)
                    act.wait_ge(mxr, 1)
                    for t, (_, n) in enumerate(TILES):
                        nc.scalar.activation(top_w[0:n, t, :], top[0:n, t, 0:TOPK], ACT.Exp, bias=nmax[0:n, t:t + 1],
                                             accum_out=tsum[0:n, t:t + 1]).then_inc(ex, 1)
                    act.wait_ge(rest_ok, 2)
                    copy(B["bias"][64:96], rest[64:96])

                @block.vector
                def _(dve):
                    step = stepper(dve, dve_chain)
                    tt_, ts_, stt = nc.vector.tensor_tensor, nc.vector.tensor_scalar, nc.vector.scalar_tensor_tensor
                    red = nc.vector.reduce_sum
                    dve.wait_ge(sq, 3)
                    for t, (_, n) in enumerate(TILES):
                        ts_(ss[0:n, t:t + 1], ss[0:n, t:t + 1], 1.0 / D, NORM_EPS, ALU.mult, ALU.add).then_inc(ms, 1)
                    dve.wait_ge(root, 3)
                    dve.wait_ge(c_in, 16 * 6)
                    for t, (_, n) in enumerate(TILES):
                        step(nc.vector.reciprocal(ss[0:n, t:t + 1], ss[0:n, t:t + 1]))
                        stt(h[0:n, t, :], x[0:n, t, :], ss[0:n, t:t + 1], gain[0:n, :], ALU.mult, ALU.mult).then_inc(hg_ok, 1)
                    dve.wait_ge(part_ok, 1)
                    tt_(rest, b, bpart[:], ALU.subtract).then_inc(rest_ok, 1)
                    step(nc.vector.memset(lg[:], 0.0))
                    step(nc.vector.memset(rank[:], 0.0))
                    for t, (_, n) in enumerate(TILES):
                        dve.wait_ge(lgd, t + 1)
                        step(tt_(lg[0:n, t, :], banks[2 + t][0:n, 0:NEXP], br[0:n, :], ALU.add))
                        step(nc.vector.max(top[:, t, :], lg[:, t, :]))
                        step(nc.vector.max_index(topi[:, t, :], top[:, t, :], lg[:, t, :]))
                    ts_(nmax[:], top[:, :, 0], -1.0, None, ALU.mult).then_inc(mxr, 1)
                    step(nc.vector.tensor_copy(topf[:], topi[:]))
                    step(tt_(oh[:], num[:, 0:NEXP].unsqueeze(1).unsqueeze(1).to_broadcast([P, 3, TOPK, NEXP]), topf[:, :, 0:TOPK].unsqueeze(3).to_broadcast([P, 3, TOPK, NEXP]), ALU.is_equal))
                    red(asg[:], oh[:].rearrange("p t k e -> p t e k"), axis=AX).then_inc(asg_ok, 1)
                    dve.wait_ge(rkd, 1)
                    step(nc.vector.tensor_copy(rank[:, 0:2, :].rearrange("p a b -> p (a b)"), banks[5][:, 0:64]))
                    step(nc.vector.tensor_copy(rank[0:TS, 2, :], banks[5][0:TS, 64:96]))
                    step(nc.vector.tensor_copy(cnt[:], banks[5][:, 96:128]))
                    step(ts_(extra[:], cnt[:], float(P), None, ALU.is_gt))
                    step(stt(extra[:], cnt[:], 2.0 * P, extra[:], ALU.is_gt, ALU.add))
                    step(nc.vector.memset(tmp[:], 1.0))
                    step(nc.vector.tensor_tensor_scan(base[:], tmp[:], extra[:], 0.0, ALU.mult, ALU.add))
                    step(nc.vector.memset(ov[:], 0.0))
                    step(nc.vector.tensor_copy(ov[:, 0:1], base[0:1, NEXP - 1:NEXP]))
                    step(tt_(base[:], base[:], extra[:], ALU.subtract))
                    step(tt_(tmp[0:1, :], base[0:1, :], extra[0:1, :], ALU.add))
                    tiles8 = num[0:1, 0:8].unsqueeze(2).to_broadcast([1, 8, NEXP])
                    by8 = lambda ap: ap.unsqueeze(1).to_broadcast([1, 8, NEXP])
                    step(tt_(wl[:, 0], by8(base[0:1, :]), tiles8, ALU.is_le))
                    step(tt_(wl[:, 1], by8(tmp[0:1, :]), tiles8, ALU.is_gt))
                    step(tt_(wl[:, 0], wl[:, 0], wl[:, 1], ALU.mult))
                    step(tt_(wl[:, 0], wl[:, 0], by8(num[0:1, 0:NEXP]), ALU.mult))
                    step(red(ov[:, 8:16], wl[:, 0], axis=AX))
                    step(nc.vector.tensor_copy(over[:], ov[:]))
                    by_k = lambda ap: ap.unsqueeze(2).to_broadcast([P, 3, TOPK, NEXP])
                    step(tt_(ohr[:], oh[:], by_k(rank[:]), ALU.mult))
                    step(red(rki[:], ohr[:], axis=AX))
                    step(tt_(ohr[:], oh[:], base[:].unsqueeze(1).unsqueeze(1).to_broadcast([P, 3, TOPK, NEXP]), ALU.mult))
                    step(red(ocol[:], ohr[:], axis=AX))
                    step(ts_(part[:], rki[:], float(P), None, ALU.is_ge))
                    step(ts_(first[:], rki[:], float(P), None, ALU.is_lt))
                    step(stt(part[:], rki[:], 2.0 * P, part[:], ALU.is_ge, ALU.add))
                    step(stt(slot[:], part[:], -float(P), rki[:], ALU.mult, ALU.add))
                    step(stt(ocol[:], part[:], -1.0, ocol[:], ALU.add, ALU.add))
                    step(stt(ocol[:], first[:], -100.0, ocol[:], ALU.mult, ALU.add))
                    last = lambda ap, n: ap.unsqueeze(3).to_broadcast([P, 3, TOPK, n])
                    step(tt_(oh[:], oh[:], last(first[:], NEXP), ALU.mult))
                    step(tt_(xeq[:], num[:, 0:8].unsqueeze(1).unsqueeze(1).to_broadcast([P, 3, TOPK, 8]), last(ocol[:], 8), ALU.is_equal))
                    for j in range(2):
                        step(tt_(cell[:, :, :, j, 0:NEXP], oh[:], last(dest[:, :, :, j], NEXP), ALU.mult))
                        step(tt_(cell[:, :, :, j, NEXP:NCHUNK], xeq[:], last(dest[:, :, :, j], 8), ALU.mult))
                    tt_(hit[:], num[:].unsqueeze(1).unsqueeze(1).to_broadcast([P, 3, TOPK, P]), last(slot[:], P), ALU.is_equal).then_inc(cell_ok, 1)
                    dve.wait_ge(part_ok, 2)
                    dve.wait_ge(rest_ok, 1)
                    tt_(rest, rest, bpart[:], ALU.subtract).then_inc(rest_ok, 1)
                    dve.wait_ge(tab, 1)
                    b7 = banks[6][:, 0:2 * NCHUNK].rearrange("p (a b) -> p a b", a=2)
                    step(ts_(empty[:], b7, 0.0, 1e6, ALU.is_equal, ALU.mult))
                    step(stt(rows_f[:], b7, -1.0, empty[:], ALU.add, ALU.add))
                    step(nc.vector.tensor_copy(src_row[:], rows_f[:, 0, :]))
                    step(nc.vector.tensor_copy(dst_row[:], rows_f[:, 1, :]))
                    dve.wait_ge(ex, 3)
                    for t, (_, n) in enumerate(TILES):
                        step(nc.vector.reciprocal(tsum[0:n, t:t + 1], tsum[0:n, t:t + 1]))
                        step(ts_(top_w[0:n, t, :], top_w[0:n, t, :], tsum[0:n, t:t + 1], None, ALU.mult))

                @block.tensor
                def _(pe):
                    mmul = nc.tensor.matmul
                    pe.wait_ge(hg_ok, 3)
                    for k in range(KD):
                        if k >= 2:
                            pe.wait_ge(hTe, k - 1)
                        for t, (t0, n) in enumerate(TILES):
                            mm = nc.tensor.transpose(banks[k % 2][:, t0:t0 + n], h[0:n, t, P * k:P * k + P], ident[0:n, 0:n])
                        mm.then_inc(hTd, 1)
                    pe.wait_ge(hTe, KD)
                    for t, (t0, n) in enumerate(TILES):
                        for k in range(KD):
                            mm = mmul(banks[2 + t][0:n, 0:NEXP], hT[:, k, t0:t0 + n], wr[:, k, :], start=(k == 0), stop=(k == KD - 1))
                        mm.then_inc(lgd, 1)
                    pe.wait_ge(asg_ok, 1)
                    for t, (t0, n) in enumerate(TILES):
                        for u in range(t + 1):
                            nu = TILES[u][1]
                            mmul(banks[5][0:n, 32 * t:32 * t + 32], rk[0:nu, 0 if u == t else 1, 0:n], asg[0:nu, u, :], start=(u == 0), stop=(u == t))
                    for u, (_, nu) in enumerate(TILES):
                        mm = mmul(banks[5][:, 96:128], rk[0:nu, 1, :], asg[0:nu, u, :], start=(u == 0), stop=(u == 2))
                    mm.then_inc(rkd, 1)
                    pe.wait_ge(cell_ok, 1)
                    for i in range(12):
                        n = TILES[i // TOPK][1]
                        mm = mmul(banks[6][:, 0:2 * NCHUNK], hit[0:n, i // TOPK, i % TOPK, :], cell[0:n, i // TOPK, i % TOPK].rearrange("p a b -> p (a b)"),
                             start=(i == 0), stop=(i == 11))
                    mm.then_inc(tab, 1)

        def experts():
            first_tiles(B, S)
            clear_semaphores()
            further_tiles(B)
            moe.close()

        def first_tiles(B, S):
            ring_in = S["ring_in"]
            l_ok = sem("ex_linear_ready")
            with nc.Block() as block:
                @block.sync
                def _(sp):
                    def up(e, wait):
                        for k in range(8):
                            if wait:
                                sp.wait_ge(S["up_used"], 8 * (e - 1) + k + 1)
                            sp.dma_start(B["ring"][:, k, :], a["w_up"][0][bass.ds(e, 1), P * k:P * k + P, :].rearrange("e p n -> (e p) n")
                                         ).then_inc(ring_in[k], 16)

                    def down(e, wait):
                        for j in range(4):
                            if wait:
                                sp.wait_ge(S["down_used"], 4 * (e - 1) + j + 1)
                            for c in range(2):
                                r0 = 256 * j + P * c
                                sp.dma_start(B["ring"][:, 8 + j, D * c:D * c + D],
                                             a["w_down"][0][bass.ds(e, 1), r0:r0 + P, :].rearrange("e p n -> (e p) n")
                                             ).then_inc(ring_in[8 + j], 16)

                    up(1, True)
                    down(0, False)
                    with sp.Fori(2, NEXP) as e:
                        up(e, True)
                        down(e - 1, True)
                    down(NEXP - 1, True)

                @block.gpsimd
                def _(pool):
                    step = stepper(pool, pool_chain)
                    last_row, last_choice = pool.to_reg(T - 1), pool.to_reg(TOPK * T - 1)

                    def gather(e, n, wait):
                        if wait:
                            pool.wait_ge(S["x_in"], 16 * e)
                        nc.gpsimd.tensor_copy(B["si"][:], src_row[:, bass.ds(e, 1)]).then_inc(S["idx"], 1)
                        pool.wait_ge(S["idx"], n)
                        if wait:
                            pool.wait_ge(S["x_turned"], e)
                        pool.nop(nofuse=True)
                        pool.indirect_dma_start(B["xg"][:], None, scratch["h"], bass.IndirectOffsetOnAxis(ap=B["si"][:, 0:1], axis=0),
                                                bounds_check=last_row, oob_is_err=False).then_inc(S["x_in"], 16)

                    def scatter(e, n):
                        nc.gpsimd.tensor_copy(B["di"][:], dst_row[:, bass.ds(e, 1)]).then_inc(S["idx"], 1)
                        pool.wait_ge(S["idx"], n)
                        pool.wait_ge(S["y_ready"], e + 1)
                        pool.nop(nofuse=True)
                        pool.indirect_dma_start(scratch["choice"], bass.IndirectOffsetOnAxis(ap=B["di"][:, 0:1], axis=0), B["y"][:], None,
                                                bounds_check=last_choice, oob_is_err=False).then_inc(S["y_out"], 16)
                        pool.wait_ge(S["y_out"], 16 * (e + 1))

                    step(nc.gpsimd.memset(B["xg"][:], 0.0))
                    gather(0, 1, False)
                    gather(1, 2, True)
                    with pool.Fori(1, NEXP) as e:
                        gather(e + 1, 2 * e + 1, True)
                        scatter(e - 1, 2 * e + 2)
                    scatter(NEXP - 1, 2 * NEXP + 1)

                @block.scalar
                def _(act):
                    def turned_x(e):
                        for i in range(2):
                            act.wait_ge(S["x_turned"], e + 1)
                            nc.scalar.activation(B["xT"][:, 4 * i:4 * i + 4, :].rearrange("p a b -> p (a b)"), banks[6 + i][:], ACT.Copy
                                                 ).then_inc(S["xT_ready"], 1)

                    def turned_h(e):
                        act.wait_ge(S["h_turned"], e + 1)
                        for i in range(2):
                            nc.scalar.activation(B["hT"][:, 4 * i:4 * i + 4, :].rearrange("p a b -> p (a b)"), banks[6 + i][:], ACT.Copy
                                                 ).then_inc(S["hT_ready"], 1)

                    def sigmoid(e):
                        act.wait_ge(S["g_ready"], e + 1)
                        nc.scalar.activation(B["sig"][:], B["g"][:], ACT.Sigmoid, scale=1.702).then_inc(S["sig_ready"], 1)

                    def rows(e, wait):
                        act.wait_ge(S["down_done"], e + 1)
                        if wait:
                            act.wait_ge(S["y_out"], 16 * e)
                        nc.scalar.activation(B["y"][:, 0:512], banks[4][:], ACT.Copy)
                        nc.scalar.activation(B["y"][:, 512:D], banks[5][:], ACT.Copy).then_inc(S["y_ready"], 1)

                    turned_x(0)
                    turned_x(1)
                    sigmoid(0)
                    turned_h(0)
                    turned_x(2)
                    sigmoid(1)
                    rows(0, False)
                    with act.Fori(2, NEXP) as e:
                        turned_h(e - 1)
                        turned_x(e + 1)
                        sigmoid(e)
                        rows(e - 1, True)
                    turned_h(NEXP - 1)
                    rows(NEXP - 1, True)

                @block.vector
                def _(dve):
                    g, lin, h = B["g"], B["lin"], B["h"]
                    with dve.Fori(0, NEXP) as e:
                        dve.wait_ge(S["up_done"], e + 1)
                        for i in range(2):
                            cs = slice(512 * i, 512 * i + 512)
                            ins = nc.vector.tensor_scalar(g[:, cs], banks[i][:], 7.0, None, ALU.min)
                        ins.then_inc(S["g_ready"], 1)
                        for i in range(2):
                            cs = slice(512 * i, 512 * i + 512)
                            ins = nc.vector.tensor_scalar(lin[:, cs], banks[2 + i][:], 7.0, -7.0, ALU.min, ALU.max)
                        ins.then_inc(S["u_read"], 1)
                        dve.wait_ge(S["g_ready"], e + 1)
                        dve.wait_ge(S["u_read"], e + 1)
                        nc.vector.scalar_tensor_tensor(lin[:], lin[:], 1.0, g[:], ALU.add, ALU.mult).then_inc(l_ok, 1)
                        dve.wait_ge(l_ok, e + 1)
                        dve.wait_ge(S["sig_ready"], e + 1)
                        nc.vector.tensor_tensor(h[:], lin[:], B["sig"][:], ALU.mult).then_inc(S["h_ready"], 1)

                @block.tensor
                def _(pe):
                    mmul = nc.tensor.matmul
                    pick_row = lambda e: B["pick"][:, bass.ds(e, 1)].to_broadcast([96, P])

                    def turn_x(e):
                        pe.wait_ge(S["x_in"], 16 * (e + 1))
                        for k in range(KD):
                            mm = nc.tensor.transpose(banks[6 + k // 4][:, P * (k % 4):P * (k % 4) + P], B["xg"][:, P * k:P * k + P], ident)
                        mm.then_inc(S["x_turned"], 1)

                    def turn_h(e):
                        pe.wait_ge(S["h_ready"], e + 1)
                        for k in range(KD):
                            mm = nc.tensor.transpose(banks[6 + k // 4][:, P * (k % 4):P * (k % 4) + P], B["h"][:, P * k:P * k + P], ident)
                        mm.then_inc(S["h_turned"], 1)

                    def up(e, wait):
                        pe.wait_ge(S["xT_ready"], 2 * (e + 1))
                        if wait:
                            pe.wait_ge(S["u_read"], e)
                        for k in range(KD):
                            if wait and k == 4:
                                turn_h(e - 1)
                            pe.wait_ge(ring_in[k], 16 * (e + 1))
                            for n in range(4):
                                mm = mmul(banks[n][:], B["xT"][:, k, :], B["ring"][:, k, 512 * n:512 * n + 512], start=(k == 0), stop=False)
                            mm.then_inc(S["up_used"], 1)
                        for n in range(4):
                            mm = mmul(banks[n][:], pick_row(e), B["bias"][:, 512 * n:512 * n + 512], start=False, stop=True)
                        mm.then_inc(S["up_done"], 1)

                    def down(e, wait):
                        pe.wait_ge(S["hT_ready"], 2 * (e + 1))
                        if wait:
                            pe.wait_ge(S["y_ready"], e)
                        for j in range(4):
                            pe.wait_ge(ring_in[8 + j], 32 * (e + 1))
                            for c in range(2):
                                for n in range(2):
                                    mm = mmul(banks[4 + n][:], B["hT"][:, 2 * j + c, :], B["ring"][:, 8 + j, D * c + 512 * n:D * c + 512 * n + 512],
                                              start=(j == 0 and c == 0), stop=False)
                            mm.then_inc(S["down_used"], 1)
                        for n in range(2):
                            mm = mmul(banks[4 + n][:], pick_row(e), B["bias"][:, 2 * FF + 512 * n:2 * FF + 512 * n + 512], start=False, stop=True)
                        mm.then_inc(S["down_done"], 1)

                    turn_x(0)
                    up(0, False)
                    turn_x(1)
                    up(1, True)
                    pe.wait_ge(S["hT_ready"], 2)
                    turn_x(2)
                    down(0, False)
                    with pe.Fori(2, NEXP) as e:
                        up(e, True)
                        pe.wait_ge(S["hT_ready"], 2 * e)
                        turn_x(e + 1)
                        down(e - 1, True)
                    pe.wait_ge(S["xT_ready"], 2 * (NEXP + 1))
                    turn_h(NEXP - 1)
                    down(NEXP - 1, True)

        def further_tiles(B):
            names = ("w", "x_in", "x_turned", "xT", "up", "g", "lin", "sig", "l", "h", "h_turned", "hT", "down", "y_ready", "y_out", "idx")
            w_in, x_in, x_turned, xT_ready, up_done, g_ready, lin_ready, sig_ready, l_ok, h_ready, h_turned, hT_ready, \
                down_done, y_ready, y_out, idx = (sem("more_" + n) for n in names)
            ring, y = B["ring"], B["y"]

            def each(eng, tile):
                with eng.If(eng.value_load(over[0:1, 0:1], min_val=0, max_val=8) > 0):
                    tile(0, eng.value_load(over[0:1, 8:9], min_val=0, max_val=NEXP - 1), True)
                    with eng.Fori(1, 8) as c:
                        tile(c, eng.value_load(over[0:1, bass.ds(c + 8, 1)], min_val=0, max_val=NEXP - 1), False)

            with nc.Block() as block:
                @block.sync
                def _(sp):
                    def tile(c, e, first):
                        if not first:
                            sp.wait_ge(down_done, c)
                        for k in range(8):
                            sp.dma_start(ring[:, k, :], a["w_up"][0][bass.ds(e, 1), P * k:P * k + P, :].rearrange("e p n -> (e p) n")).then_inc(w_in, 16)
                            sp.dma_start(ring[:, 8 + k // 2, D * (k % 2):D * (k % 2) + D],
                                         a["w_down"][0][bass.ds(e, 1), P * k:P * k + P, :].rearrange("e p n -> (e p) n")).then_inc(w_in, 16)
                    each(sp, tile)

                @block.gpsimd
                def _(pool):
                    last_row, last_choice = pool.to_reg(T - 1), pool.to_reg(TOPK * T - 1)

                    def tile(c, e, first):
                        nc.gpsimd.tensor_copy(B["si"][:], src_row[:, bass.ds(c + NEXP, 1)]).then_inc(idx, 1)
                        nc.gpsimd.tensor_copy(B["di"][:], dst_row[:, bass.ds(c + NEXP, 1)]).then_inc(idx, 1)
                        pool.wait_ge(idx, 2 * (c + 1))
                        pool.nop(nofuse=True)
                        pool.indirect_dma_start(B["xg"][:], None, scratch["h"], bass.IndirectOffsetOnAxis(ap=B["si"][:, 0:1], axis=0),
                                                bounds_check=last_row, oob_is_err=False).then_inc(x_in, 16)
                        pool.wait_ge(x_in, 16 * (c + 1))
                        pool.wait_ge(y_ready, 2 * (c + 1))
                        pool.nop(nofuse=True)
                        pool.indirect_dma_start(scratch["choice"], bass.IndirectOffsetOnAxis(ap=B["di"][:, 0:1], axis=0), y[:], None,
                                                bounds_check=last_choice, oob_is_err=False).then_inc(y_out, 16)
                        pool.wait_ge(y_out, 16 * (c + 1))
                        pool.nop(nofuse=True)
                    each(pool, tile)

                @block.scalar
                def _(act):
                    def tile(c, e, first):
                        for done, dst, ready in ((x_turned, B["xT"], xT_ready), (h_turned, B["hT"], hT_ready)):
                            if dst is B["hT"]:
                                act.wait_ge(g_ready, 2 * (c + 1))
                                nc.scalar.activation(B["sig"][:], B["g"][:], ACT.Sigmoid, scale=1.702).then_inc(sig_ready, 1)
                            for i in range(2):
                                act.wait_ge(done, c + 1)
                                nc.scalar.activation(dst[:, 4 * i:4 * i + 4, :].rearrange("p a b -> p (a b)"), banks[6 + i][:], ACT.Copy).then_inc(ready, 1)
                        act.wait_ge(down_done, c + 1)
                        for i in range(2):
                            nc.scalar.activation(y[:, 512 * i:512 * i + 512], banks[4 + i][:], ACT.Copy).then_inc(y_ready, 1)
                    each(act, tile)

                @block.vector
                def _(dve):
                    def tile(c, e, first):
                        dve.wait_ge(up_done, c + 1)
                        for i in range(2):
                            cs = slice(512 * i, 512 * i + 512)
                            nc.vector.tensor_scalar(B["g"][:, cs], banks[i][:], 7.0, None, ALU.min).then_inc(g_ready, 1)
                            nc.vector.tensor_scalar(B["lin"][:, cs], banks[2 + i][:], 7.0, -7.0, ALU.min, ALU.max).then_inc(lin_ready, 1)
                        dve.wait_ge(g_ready, 2 * (c + 1))
                        dve.wait_ge(lin_ready, 2 * (c + 1))
                        nc.vector.scalar_tensor_tensor(B["lin"][:], B["lin"][:], 1.0, B["g"][:], ALU.add, ALU.mult).then_inc(l_ok, 1)
                        dve.wait_ge(l_ok, c + 1)
                        dve.wait_ge(sig_ready, c + 1)
                        nc.vector.tensor_tensor(B["h"][:], B["lin"][:], B["sig"][:], ALU.mult).then_inc(h_ready, 1)
                    each(dve, tile)

                @block.tensor
                def _(pe):
                    mmul = nc.tensor.matmul

                    def tile(c, e, first):
                        def turn(src, done):
                            for k in range(KD):
                                mm = nc.tensor.transpose(banks[6 + k // 4][:, P * (k % 4):P * (k % 4) + P], src[:, P * k:P * k + P], ident)
                            mm.then_inc(done, 1)
                        pick_row = B["pick"][:, bass.ds(e, 1)].to_broadcast([96, P])
                        pe.wait_ge(x_in, 16 * (c + 1))
                        turn(B["xg"], x_turned)
                        pe.wait_ge(xT_ready, 2 * (c + 1))
                        pe.wait_ge(w_in, 256 * (c + 1))
                        for n in range(4):
                            for k in range(KD):
                                mmul(banks[n][:], B["xT"][:, k, :], ring[:, k, 512 * n:512 * n + 512], start=(k == 0), stop=False)
                            mm = mmul(banks[n][:], pick_row, B["bias"][:, 512 * n:512 * n + 512], start=False, stop=True)
                        mm.then_inc(up_done, 1)
                        pe.wait_ge(h_ready, c + 1)
                        turn(B["h"], h_turned)
                        pe.wait_ge(hT_ready, 2 * (c + 1))
                        for n in range(2):
                            for k in range(KD):
                                mmul(banks[4 + n][:], B["hT"][:, k, :], ring[:, 8 + k // 2, D * (k % 2) + 512 * n:D * (k % 2) + 512 * n + 512],
                                     start=(k == 0), stop=False)
                            mm = mmul(banks[4 + n][:], pick_row, B["bias"][:, 2 * FF + 512 * n:2 * FF + 512 * n + 512], start=False, stop=True)
                        mm.then_inc(down_done, 1)
                    each(pe, tile)

        def finish():
            with nc.Block() as block, ExitStack() as st:
                rows = sb(st, "choice_rows", [P, 3, TOPK, D])
                gain = sb(st, "final_gain", [P, D])
                sq_out, ss = sb(st, "final_sq", [P, D]), sb(st, "final_ss", [P, 3])
                r_in, g_in, x_ok, sq, ms, root, y_ok = ([sem(f"fin_rows{t}") for t in range(3)], *(sem("fin_" + n) for n in (
                    "gain_in", "x_ready", "squares", "ms", "root", "y_ready")))

                @block.sync
                def _(sp):
                    for t, (t0, n) in enumerate(TILES):
                        sp.dma_start(rows[0:n, t], scratch["choice"][TOPK * t0:TOPK * (t0 + n), :].rearrange("(t k) d -> t k d", k=TOPK)).then_inc(r_in[t], 16)
                    sp.dma_start(gain[:], bass.AP(a["norm_final"].tensor, 0, [[0, P], [1, D]])).then_inc(g_in, 16)
                    for t, (t0, n) in enumerate(TILES):
                        sp.wait_ge(y_ok, t + 1)
                        dst = o["y_p"][0, t0:t0 + n, :] if t < 2 else o["y_s"][:, 0, :]
                        sp.dma_start(dst, x[0:n, t, :]).then_inc(outs.sem, 16)
                        outs.n += 16

                @block.scalar
                def _(act):
                    for t, (_, n) in enumerate(TILES):
                        act.wait_ge(x_ok, t + 1)
                        if t:
                            act.wait_ge(sq, t)
                        nc.scalar.activation(sq_out[0:n, :], x[0:n, t, :], ACT.Square, accum_out=ss[0:n, t:t + 1]).then_inc(sq, 1)
                    act.wait_ge(ms, 3)
                    for t, (_, n) in enumerate(TILES):
                        nc.scalar.activation(ss[0:n, t:t + 1], ss[0:n, t:t + 1], ACT.Sqrt).then_inc(root, 1)

                @block.vector
                def _(dve):
                    step = stepper(dve, dve_chain)
                    stt = nc.vector.scalar_tensor_tensor
                    for t, (_, n) in enumerate(TILES):
                        dve.wait_ge(r_in[t], 16)
                        for k in range(TOPK):
                            ins = stt(x[0:n, t, :], rows[0:n, t, k, :], top_w[0:n, t, k:k + 1], x[0:n, t, :], ALU.mult, ALU.add)
                            if k < TOPK - 1:
                                step(ins)
                        ins.then_inc(x_ok, 1)
                    for t, (_, n) in enumerate(TILES):
                        dve.wait_ge(sq, t + 1)
                        nc.vector.tensor_scalar(ss[0:n, t:t + 1], ss[0:n, t:t + 1], 1.0 / D, NORM_EPS, ALU.mult, ALU.add).then_inc(ms, 1)
                    dve.wait_ge(g_in, 16)
                    dve.wait_ge(root, 3)
                    for t, (_, n) in enumerate(TILES):
                        step(nc.vector.reciprocal(ss[0:n, t:t + 1], ss[0:n, t:t + 1]))
                        stt(x[0:n, t, :], x[0:n, t, :], ss[0:n, t:t + 1], gain[0:n, :], ALU.mult, ALU.mult).then_inc(y_ok, 1)

        project()
        rwkv()
        clear_semaphores()
        compress()
        attend()
        clear_semaphores()
        merge()
        expert_buffers()
        route()
        experts()
        finish()
        with nc.Block() as block:
            @block.sync
            def _(sp):
                sp.wait_ge(win_copied, 16)
                sp.wait_ge(outs.sem, outs.n)



CONST_NAMES = ("c_masks", "c_carry", "c_hot", "c_cmp_seen", "c_cols", "c_group", "c_own", "c_blk", "c_numbers", "c_rank", "c_dest", "c_pick")
SCRATCH = [("rwkv_in", (6, TS, 512), F32), ("rwkv_out", (TS, 512), F32),
           ("cmp_rows", (TP, 256), F32), ("kv_s", (TS, 768), F32), ("bias", (8, NX), F32), ("gate_s", (TS, 24), F32),
           ("yb_s", (TS, 512), F32), ("h", (T, D), F32), ("choice", (TOPK * T, D), F32)]


INS = ['x_prompt', 'x_sample', 'cache_cmp_kv', 'cache_sel_kv', 'state_win_kv', 'state_rwkv', 'state_rwkv_shift', 'page_table',
       'norm_attn', 'w_in', 'mu_shift', 'w0', 'w_decay_up', 'a0', 'w_iclr_up', 'w_gate_up', 'k_k', 'k_a', 'r_k', 'ln_x_w', 'ln_x_b',
       'pe_cmp_k', 'pe_cmp_v', 'w_cmp_k1', 'w_cmp_k2', 'w_cmp_v1', 'w_cmp_v2', 'rel_bias', 'w_br_a', 'w_br_b', 'w_out', 'norm_ffn',
       'w_router', 'b_router', 'w_up', 'b_up', 'w_down', 'b_down', 'norm_final']
OUTS = [('y_p', (1, TP, D)), ('y_s', (TS, 1, D)), ('cmp_p', (1, 1, TP, 2, 2, HD)), ('sel_p', (1, 1, TP, 2, 2, HD)),
        ('win_p', (1, 1, TP, 2, 2, HD)), ('wkv_p', (1, 1, 8, HD, HD)), ('shift_p', (1, 1, AP_COLS)),
        ('cmp_s', (1, TS, 1, 2, 2, HD)), ('sel_s', (1, TS, 1, 2, 2, HD)), ('win_s', (1, TS, 512, 2, 2, HD)),
        ('wkv_s', (1, TS, 8, HD, HD)), ('shift_s', (1, TS, AP_COLS))]


def kernel(**inputs):
    import concourse.bacc as bacc
    from concourse.bass_utils import run_bass_kernel_spmd

    nc = bacc.Bacc("TRN2", target_bir_lowering=False, num_devices=1)
    arrays, a, o = {}, {}, {}
    consts = dict(zip(CONST_NAMES, shape_constants()))
    for name, v in [(n, inputs[n]) for n in INS] + list(consts.items()):
        v = np.ascontiguousarray(v)
        arrays[f"in_{name}"] = v
        a[name] = nc.dram_tensor(f"in_{name}", v.shape, mybir.dt.from_np(v.dtype), kind="ExternalInput").ap()
    for name, shape in OUTS:
        o[name] = nc.dram_tensor(f"out_{name}", shape, F32, kind="ExternalOutput").ap()
    scratch = {name: nc.dram_tensor(f"scratch_{name}", shape, dt).ap() for name, shape, dt in SCRATCH}
    build(nc, a, o, scratch)
    r = run_bass_kernel_spmd(nc, [arrays], core_ids=[0])
    return tuple(r.results[0][f"out_{name}"] for name, _ in OUTS)
```
